# Optimizing a Trainium2 kernel written in Bass

```python
import math
import jax, jax.numpy as jnp
from jax import lax
import numpy as np

D_MODEL = 1024
BATCH = 1
SEQ = 1024
DEPTH = 2
DEC_BATCH = 8
DEC_SEQ = 16
PAST_LEN = 512

CHUNK = 64
N_MIXERS = 2
N_HGRN_LAYERS = (DEPTH + 1) // 2
N_GLA_LAYERS = DEPTH // 2
HGRN_EXPAND = 128
HGRN_HEADS = D_MODEL // HGRN_EXPAND
HGRN_DK = HGRN_EXPAND
HGRN_DV = D_MODEL // HGRN_HEADS
HGRN_FDIM = HGRN_HEADS * HGRN_DK
GLA_HEADS = 4
GLA_KEY_DIM = D_MODEL // 2
GLA_VAL_DIM = D_MODEL
GLA_DK = GLA_KEY_DIM // GLA_HEADS
GLA_DV = GLA_VAL_DIM // GLA_HEADS
GLA_GATE_RANK = 16
GLA_GATE_NORMALIZER = 16.0
D_FF = 2816
CONV_WIDTH = 3
ALPHA = (2.0 * DEPTH) ** 0.25
BETA = (8.0 * DEPTH) ** -0.25
LN_EPS = 1e-5
RMS_EPS = 1e-6

kernel_name = "hgrn2_gla_convffn_streaming_step"

def layer_norm(x, g, b):
    xf = x.astype(jnp.float32)
    mu = jnp.mean(xf, axis=-1, keepdims=True)
    xc = xf - mu
    var = jnp.mean(xc * xc, axis=-1, keepdims=True)
    return (xc * lax.rsqrt(var + LN_EPS) * g.astype(jnp.float32) + b.astype(jnp.float32)).astype(x.dtype)

def rms_norm(x, g):
    xf = x.astype(jnp.float32)
    ms = jnp.mean(xf * xf, axis=-1, keepdims=True)
    return xf * lax.rsqrt(ms + RMS_EPS) * g.astype(jnp.float32)

def chunked_gated_linear_attention(q, k, v, logf, s0, chunk):
    B, T, H, DK = q.shape
    DV = v.shape[-1]
    n = T // chunk

    def blocks(a):
        return a.astype(jnp.float32).reshape(B, n, chunk, H, a.shape[-1]).transpose(1, 0, 3, 2, 4)

    causal = jnp.tril(jnp.ones((chunk, chunk), dtype=bool))[:, :, None]

    def step(S, inp):
        qc, kc, vc, gc = inp
        b = jnp.cumsum(gc, axis=2)
        diff = b[:, :, :, None, :] - b[:, :, None, :, :]
        decay = jnp.exp(jnp.where(causal, diff, -jnp.inf))
        scores = jnp.einsum('bhtd,bhsd,bhtsd->bhts', qc, kc, decay)
        o = (jnp.einsum('bhts,bhsv->bhtv', scores, vc)
             + jnp.einsum('bhtd,bhdv->bhtv', qc * jnp.exp(b), S))
        b_last = b[:, :, -1, :]
        S_new = (jnp.exp(b_last)[..., None] * S
                 + jnp.einsum('bhsd,bhsv->bhdv', kc * jnp.exp(b_last[:, :, None, :] - b), vc))
        return S_new, o

    S_fin, o = lax.scan(step, s0.astype(jnp.float32), (blocks(q), blocks(k), blocks(v), blocks(logf)))
    o = o.transpose(1, 0, 3, 2, 4).reshape(B, T, H, DV)
    return o, S_fin

def hgrn2_mixer(x, s0, lb, w_in, w_out, norm_g, chunk):
    B, T, _ = x.shape
    proj = x @ w_in
    q, fz, i, g = jnp.split(proj, [HGRN_FDIM, 2 * HGRN_FDIM, 3 * HGRN_FDIM], axis=-1)
    q = jax.nn.silu(q.astype(jnp.float32)).reshape(B, T, HGRN_HEADS, HGRN_DK)
    lbh = lb.reshape(HGRN_HEADS, HGRN_DK)
    f = lbh + (1.0 - lbh) * jax.nn.sigmoid(fz.astype(jnp.float32).reshape(B, T, HGRN_HEADS, HGRN_DK))
    logf = jnp.log(f)
    k = 1.0 - f
    v = i.reshape(B, T, HGRN_HEADS, HGRN_DV)
    o, s_new = chunked_gated_linear_attention(q, k, v, logf, s0, chunk)
    gate = jax.nn.silu(g.astype(jnp.float32)).reshape(B, T, HGRN_HEADS, HGRN_DV)
    o = (rms_norm(o, norm_g) * gate).astype(x.dtype).reshape(B, T, D_MODEL)
    return o @ w_out, s_new.astype(s0.dtype)

def gla_mixer(x, s0, w_in, w_gk2, b_gk2, w_out, norm_g, chunk):
    B, T, _ = x.shape
    proj = x @ w_in
    s1 = GLA_KEY_DIM
    s2 = 2 * GLA_KEY_DIM
    s3 = s2 + GLA_VAL_DIM
    s4 = s3 + GLA_VAL_DIM
    q, k, v, g, r = jnp.split(proj, [s1, s2, s3, s4], axis=-1)
    q = q.reshape(B, T, GLA_HEADS, GLA_DK) * (GLA_DK ** -0.5)
    k = k.reshape(B, T, GLA_HEADS, GLA_DK)
    v = v.reshape(B, T, GLA_HEADS, GLA_DV)
    gk = jax.nn.log_sigmoid((r @ w_gk2 + b_gk2).astype(jnp.float32)) / GLA_GATE_NORMALIZER
    gk = gk.reshape(B, T, GLA_HEADS, GLA_DK)
    o, s_new = chunked_gated_linear_attention(q, k, v, gk, s0, chunk)
    gate = jax.nn.silu(g.astype(jnp.float32)).reshape(B, T, GLA_HEADS, GLA_DV)
    o = (rms_norm(o, norm_g) * gate).astype(x.dtype).reshape(B, T, GLA_VAL_DIM)
    return o @ w_out, s_new.astype(s0.dtype)

def conv_ffn(x, prev, w_up, conv_w, conv_b, w_down):
    L = x.shape[1]
    a, b = jnp.split(x @ w_up, 2, axis=-1)
    a_full = jnp.concatenate([prev.astype(a.dtype), a], axis=1)
    conv = conv_b
    for j in range(CONV_WIDTH):
        conv = conv + a_full[:, j:j + L] * conv_w[j]
    h = jax.nn.gelu(conv) * b
    return h @ w_down, a_full[:, -(CONV_WIDTH - 1):]

def run_trunk(x, st_hgrn, st_gla, st_conv, chunk, lb_all,
              hgrn_w_in, hgrn_w_out, hgrn_norm_g,
              gla_w_in, gla_w_gk2, gla_b_gk2, gla_w_out, gla_norm_g,
              ln_mix_g, ln_mix_b, ffn_w_up, ffn_conv_w, ffn_conv_b, ffn_w_down,
              ln_ffn_g, ln_ffn_b):
    new_h, new_g, new_c = [], [], []
    for i in range(DEPTH):
        j = i // N_MIXERS
        if i % N_MIXERS == 0:
            m, s = hgrn2_mixer(x, st_hgrn[j], lb_all[i], hgrn_w_in[j], hgrn_w_out[j], hgrn_norm_g[j], chunk)
            new_h.append(s)
        else:
            m, s = gla_mixer(x, st_gla[j], gla_w_in[j], gla_w_gk2[j], gla_b_gk2[j], gla_w_out[j], gla_norm_g[j], chunk)
            new_g.append(s)
        x = layer_norm(ALPHA * x + m, ln_mix_g[i], ln_mix_b[i])
        f, c = conv_ffn(x, st_conv[i], ffn_w_up[i], ffn_conv_w[i], ffn_conv_b[i], ffn_w_down[i])
        new_c.append(c)
        x = layer_norm(ALPHA * x + f, ln_ffn_g[i], ln_ffn_b[i])
    return x, jnp.stack(new_h), jnp.stack(new_g), jnp.stack(new_c)

def setup_inputs(seed: int = 0) -> dict:
    key = jax.random.key(seed)
    ks = jax.random.split(key, 24)
    f32 = jnp.float32
    D = D_MODEL
    hgrn_cols = 3 * HGRN_FDIM + D
    hgrn_scale = jnp.concatenate([jnp.ones((2 * HGRN_FDIM,), f32), jnp.full((D,), BETA, f32), jnp.ones((D,), f32)])
    gla_cols = 2 * GLA_KEY_DIM + 2 * GLA_VAL_DIM + GLA_GATE_RANK
    gla_scale = jnp.concatenate([jnp.ones((2 * GLA_KEY_DIM,), f32), jnp.full((GLA_VAL_DIM,), BETA, f32),
                                 jnp.ones((GLA_VAL_DIM + GLA_GATE_RANK,), f32)])
    inputs = {
        "x_prompt": jax.random.normal(ks[0], (BATCH, SEQ, D), f32),
        "x_sample": jax.random.normal(ks[1], (DEC_BATCH, DEC_SEQ, D), f32),
        "state_hgrn": 0.5 * jax.random.normal(ks[2], (N_HGRN_LAYERS, DEC_BATCH, HGRN_HEADS, HGRN_DK, HGRN_DV), f32),
        "state_gla": 0.5 * jax.random.normal(ks[3], (N_GLA_LAYERS, DEC_BATCH, GLA_HEADS, GLA_DK, GLA_DV), f32),
        "state_ffn_conv": jax.random.normal(ks[4], (DEPTH, DEC_BATCH, CONV_WIDTH - 1, D_FF), f32),
        "lb_param": 0.1 * jax.random.normal(ks[5], (DEPTH + 1, HGRN_FDIM), f32),
        "hgrn_w_in": jax.random.normal(ks[6], (N_HGRN_LAYERS, D, hgrn_cols), f32) * (D ** -0.5) * hgrn_scale,
        "hgrn_w_out": jax.random.normal(ks[7], (N_HGRN_LAYERS, D, D), f32) * (D ** -0.5) * BETA,
        "hgrn_norm_g": 1.0 + 0.01 * jax.random.normal(ks[8], (N_HGRN_LAYERS, HGRN_DV), f32),
        "gla_w_in": jax.random.normal(ks[9], (N_GLA_LAYERS, D, gla_cols), f32) * (D ** -0.5) * gla_scale,
        "gla_w_gk2": jax.random.normal(ks[10], (N_GLA_LAYERS, GLA_GATE_RANK, GLA_KEY_DIM), f32) * (GLA_GATE_RANK ** -0.5),
        "gla_b_gk2": 0.01 * jax.random.normal(ks[11], (N_GLA_LAYERS, GLA_KEY_DIM), f32),
        "gla_w_out": jax.random.normal(ks[12], (N_GLA_LAYERS, GLA_VAL_DIM, D), f32) * (GLA_VAL_DIM ** -0.5) * BETA,
        "gla_norm_g": 1.0 + 0.01 * jax.random.normal(ks[13], (N_GLA_LAYERS, GLA_DV), f32),
        "ln_mix_g": 1.0 + 0.01 * jax.random.normal(ks[14], (DEPTH, D), f32),
        "ln_mix_b": 0.01 * jax.random.normal(ks[15], (DEPTH, D), f32),
        "ffn_w_up": jax.random.normal(ks[16], (DEPTH, D, 2 * D_FF), f32) * (D ** -0.5),
        "ffn_conv_w": jax.random.normal(ks[17], (DEPTH, CONV_WIDTH, D_FF), f32) * (CONV_WIDTH ** -0.5),
        "ffn_conv_b": 0.01 * jax.random.normal(ks[18], (DEPTH, D_FF), f32),
        "ffn_w_down": jax.random.normal(ks[19], (DEPTH, D_FF, D), f32) * (D_FF ** -0.5) * BETA,
        "ln_ffn_g": 1.0 + 0.01 * jax.random.normal(ks[20], (DEPTH, D), f32),
        "ln_ffn_b": 0.01 * jax.random.normal(ks[21], (DEPTH, D), f32),
    }
    return inputs

def reference(x_prompt, x_sample, state_hgrn, state_gla, state_ffn_conv, lb_param,
              hgrn_w_in, hgrn_w_out, hgrn_norm_g,
              gla_w_in, gla_w_gk2, gla_b_gk2, gla_w_out, gla_norm_g,
              ln_mix_g, ln_mix_b, ffn_w_up, ffn_conv_w, ffn_conv_b, ffn_w_down,
              ln_ffn_g, ln_ffn_b):
    lb_all = jnp.cumsum(jax.nn.softmax(lb_param.astype(jnp.float32), axis=0), axis=0)
    weights = (hgrn_w_in, hgrn_w_out, hgrn_norm_g, gla_w_in, gla_w_gk2, gla_b_gk2, gla_w_out, gla_norm_g,
               ln_mix_g, ln_mix_b, ffn_w_up, ffn_conv_w, ffn_conv_b, ffn_w_down, ln_ffn_g, ln_ffn_b)
    dt = x_prompt.dtype
    z_hgrn = jnp.zeros((N_HGRN_LAYERS, BATCH, HGRN_HEADS, HGRN_DK, HGRN_DV), dt)
    z_gla = jnp.zeros((N_GLA_LAYERS, BATCH, GLA_HEADS, GLA_DK, GLA_DV), dt)
    z_conv = jnp.zeros((DEPTH, BATCH, CONV_WIDTH - 1, D_FF), dt)
    y_prompt, hgrn_p, gla_p, conv_p = run_trunk(x_prompt, z_hgrn, z_gla, z_conv, CHUNK, lb_all, *weights)
    y_sample, hgrn_s, gla_s, conv_s = run_trunk(x_sample, state_hgrn, state_gla, state_ffn_conv,
                                                x_sample.shape[1], lb_all, *weights)
    return (y_prompt, y_sample, hgrn_p, hgrn_s, gla_p, gla_s, conv_p, conv_s)


_drawn_inputs = setup_inputs


def setup_inputs(seed=0):
    import zlib

    import numpy as np

    out = dict(_drawn_inputs(seed))
    spreads = {}
    factors = {'hgrn_norm_g': 8.0,
     'gla_b_gk2': 21.834,
     'gla_norm_g': 39.802,
     'ln_mix_g': 3.677,
     'ln_mix_b': 3.526,
     'ffn_conv_b': 8.0,
     'ln_ffn_g': 3.857,
     'ln_ffn_b': 3.716}
    for name, (base, spread) in spreads.items():
        noise = np.random.default_rng([zlib.crc32(name.encode()), seed]).standard_normal(out[name].shape)
        drawn = base * np.exp(spread * noise) if base else spread * noise
        out[name] = __import__('jax').numpy.asarray(drawn.astype(out[name].dtype))
    for name, factor in factors.items():
        out[name] = (out[name] * factor).astype(out[name].dtype)
    return out
```

```python
import concourse.bass as bass
from concourse import mybir
from contextlib import ExitStack

P = 128
D = 1024
KD = D // P
PROMPT, STREAMS, STREAM_T = 1024, 8, 16
T = PROMPT + STREAMS * STREAM_T
NT = T // P
PT = PROMPT // P
CH = 384
NC = T // CH
TPC = CH // P
FF = 2816
NFF = FF // P
GROUPS = NFF // 2
DOWN_ALL = GROUPS * 2 * NT + 1
HEADS_H, HEADS_G = 8, 4
DV_H, DV_G = 128, 256
RANK = 16
ALPHA = 4.0 ** 0.25
LN_EPS, RMS_EPS = 1e-5, 1e-6
LEVELS = [64, 32, 16, 8, 4, 2, 1]
NL = len(LEVELS)
DEC_FROM = LEVELS.index(STREAM_T // 2)
UNIT = 1024
ROWS = 2 * STREAMS + 4
TAILS = 2 + 2 * STREAMS

JOB_O = (2 * NT, 8 * NT)
JOB_F = (4 * NT, 10 * NT)
JOB_G = 6 * NT

U_H = 0
U_WH = U_H + 4 * HEADS_H
U_F0 = U_WH + 8
U_R = U_F0 + 6 * GROUPS
U_G = U_R + 1
U_WG = U_G + 6 * HEADS_G
U_F1 = U_WG + 8


class Signal:

    def __init__(self, sem, per, base=0):
        self.sem, self.per, self.base = sem, per, base

    def at(self, i, k):
        return i * self.per + (self.base + k)

    def layer(self, n, passes):
        return Signal(self.sem, self.per, n * self.per * passes)


def build(nc, A, out):
    F32, F32R, U8 = mybir.dt.float32, mybir.dt.float32r, mybir.dt.uint8
    ALU, ACT = mybir.AluOpType, mybir.ActivationFunctionType
    AX = mybir.AxisListType

    with ExitStack() as ctx:
        ctx.enter_context(nc.allow_non_contiguous_dma(reason="small parameters"))

        cursor = [1152]

        def place(name, shape, dt, offset=None):
            size = (4 if dt != U8 else 1)
            for s in shape[1:]:
                size *= s
            size = -(-size // 32) * 32
            if offset is None:
                offset = cursor[0]
                cursor[0] += size
            return nc.alloc_sbuf_tensor_at(name, shape, dt, offset=offset)

        ident = place("ident", [P, P], F32)
        level_mask = place("level_mask", [P, NL * 64], U8)
        keep = place("keep", [P, T], U8)
        own_stream = place("own_stream", [P, STREAMS], F32)
        ones = place("ones", [P, 1], F32)
        eps_ln = place("eps_ln", [P, 1], F32)
        eps_rms = place("eps_rms", [P, 1], F32)
        stats = place("stats", [P, 2, 2, 6], F32)
        moments = place("moments", [P, NT, 2], F32)
        log_var = place("log_var", [P, NT], F32)
        inv_std = place("inv_std", [P, NT], F32)

        xt_hi = place("xt_hi", [P, KD, T], F32R)
        xt_lo = place("xt_lo", [P, KD, T], F32R)
        tm = place("tm", [P, NT, D], F32)
        ring_hi, ring_lo, ring_raw = [], [], []
        for s in range(6):
            ring_hi.append(place(f"ring_hi{s}", [P, UNIT], F32R))
            at = cursor[0]
            ring_lo.append(place(f"ring_lo{s}", [P, UNIT], F32R))
            ring_raw.append(place(f"ring_raw{s}", [P, UNIT], F32, at))
        work = cursor[0]

        att = {}

        def attention_tiles(n, dv, head0):
            cursor[0] = work
            t = {}
            for name in ("q", "qh", "k", "b", "c0", "c1"):
                t[name] = place(f"{n}_{name}", [P, T], F32)
            kt_at = work + 2 * T * 4
            t["kt"] = place(f"{n}_kt", [P, NT, P], F32, kt_at)
            t["vz"] = place(f"{n}_vz", [P, STREAMS, dv], F32, work + 4 * T * 4)
            t["a"] = place(f"{n}_a", [P, NT, P], F32)
            t["v"] = place(f"{n}_v", [P, NT, dv], F32)
            at = cursor[0]
            t["chain"] = place(f"{n}_chain", [P, PT, dv], F32)
            t["e"] = place(f"{n}_e", [P, T], F32, at)
            cursor[0] = max(cursor[0], at + T * 4)
            t["s0"] = place(f"{n}_s0", [P, STREAMS, dv], F32)
            t["qz"] = place(f"{n}_qz", [P, STREAMS, P], F32)
            if n == "h":
                t["gt"] = place("h_gt", [P, NT, dv], F32)
                t["lb"] = place("h_lb", [P, HEADS_H, 3], F32)
                t["lbx"] = place("h_lbx", [P, HEADS_H, 3], F32)
                t["lbs"] = place("h_lbs", [P, HEADS_H, 1], F32)
                t["floor"] = place("h_floor", [P, HEADS_H, 1], F32)
                t["span"] = place("h_span", [P, HEADS_H, 1], F32)
            else:
                t["wgk"] = place("g_wgk", [RANK, P], F32)
                t["bgk"] = place("g_bgk", [P, HEADS_G], F32)
                t["bcol"] = place("g_bcol", [P, 1], F32)
            t["norm"] = place(f"{n}_norm", [P, dv], F32)
            t["junk"] = place(f"{n}_junk", [P, dv], F32)
            t["dec"] = place(f"{n}_dec", [P, 2 * STREAMS], F32)
            t["dot"] = place(f"{n}_dot", [P, NT], F32)
            t["ss"] = place(f"{n}_ss", [P, NT], F32)
            t["lss"] = place(f"{n}_lss", [P, NT], F32)
            t["rstd"] = place(f"{n}_rstd", [P, NT], F32)
            assert cursor[0] <= nc.sbuf_usable_end, (n, cursor[0])
            att[n] = t

        attention_tiles("h", DV_H, 0)
        attention_tiles("g", DV_G, 0)
        rt = tm[0:RANK, :, D - P:D]

        level_f32 = place("level_f32", [P, NL * 64], F32, work)
        keep_f32 = place("keep_f32", [P, T], F32, work + T * 4)

        cursor[0] = work
        h_at = cursor[0]
        h_hi, h_lo = [], []
        for g in range(2):
            h_hi.append([place(f"h_hi{g}{u}", [P, T], F32R) for u in range(2)])
            h_lo.append([place(f"h_lo{g}{u}", [P, T], F32R) for u in range(2)])
        rows_in = place("rows_in", [ROWS, FF], F32, h_at)
        tails_out = place("tails_out", [TAILS, FF], F32, h_at + 4 * 4 * T)
        ax_at = cursor[0]
        ax = [place(f"ax{u}", [P, 2 + PROMPT + STREAMS * (2 + STREAM_T)], F32) for u in range(2)]
        cv = [place(f"cv{u}", [P, T], F32) for u in range(2)]
        params = place("params", [P, NFF, ROWS], F32)
        tails = place("tails", [P, NFF, TAILS], F32)
        assert cursor[0] <= nc.sbuf_usable_end, cursor[0]
        ln_att = [place(f"ln_att{j}", [P, D], F32, work + 3 * T * 4 + j * D * 4) for j in range(2)]
        ln_ffn = [place(f"ln_ffn{j}", [P, D], F32, ax_at + j * D * 4) for j in range(2)]

        bank = [ctx.enter_context(nc.psum_tensor(f"bank{i}", [P, 512], F32)) for i in range(8)]
        x2_dram = nc.dram_tensor("x2_scratch", (T, D), F32, kind="Internal").ap()

        def sem(name):
            return ctx.enter_context(nc.semaphore(name))

        const_in = sem("const_in")
        x_in = [sem(f"x_in{t}") for t in range(NT)]
        slot_in = [sem(f"slot_in{s}") for s in range(6)]
        unit_hi = sem("unit_hi")
        unit_split = sem("unit_split")
        tj_done = sem("tj_done")
        tj_hi = sem("tj_hi")
        tj_lo = sem("tj_lo")
        w_done = sem("w_done")
        w_added = sem("w_added")
        ln_moments = sem("ln_moments")
        ln_log = sem("ln_log")
        ln_std = sem("ln_std")
        ln_step = sem("ln_step")
        ln_a = sem("ln_apply")
        ln_done = sem("ln_done")
        res_in = [sem(f"res_in{t}") for t in range(NT)]
        x2_out = sem("x2_out")
        y_out = sem("y_out")
        lnrow_in = sem("lnrow_in")
        prep = sem("prep")
        start_dve = sem("start_dve")
        start_pool = sem("start_pool")

        def attention_signals(n, dv):
            npj = PT * dv // 512
            s = dict(
                q_proj=3, k_proj=3, z_proj=3, q_sig=3, k_sig=3, q_ready=3, k_ready=1, g_act=1,
                log_f=1, z_abs=3, z_min=3, z_exp=1, z_log=1, scan_in=1, scanned=1,
                sub=NL, exp=NL, lvl=NL, lvl_pe=NL, pred=2 * NL + NL - DEC_FROM, e=1, dec=1, prod=1, qh=1, qz=1, kh_sub=2, kh_exp=1,
                kh=1, kt_pe=3, kt=3, dots_pe=1, dots=1, vz=1, kvp_pe=npj, chain=PT, odec_pe=1,
                kvd_pe=npj, s0new=STREAMS, o_pe=npj, o_add=NT, squares=NT, lss=1, rstd=1, gated_o=1, final=1,
                gated=2 if n == "h" else 1, vg_pe=NT, vg=NT, forget=2,
            )
            s.update(s0_in=16, state_out=16, stream_out=16)
            only = dict(h=("q_sig", "k_sig", "log_f", "forget"),
                        g=("z_proj", "z_abs", "z_min", "z_exp", "z_log", "scan_in", "k_ready"))
            s = {k: v for k, v in s.items() if k not in only["g" if n == "h" else "h"]}
            if n == "g":
                s.update(wgk_in=16, r_pe=3, rt=3, bcol=1)
            return s

        SIG = {"h": {k: Signal(sem(f"att_{k}"), v) for k, v in attention_signals("h", DV_H).items()}, "g": {}}
        for k, v in attention_signals("g", DV_G).items():
            old = SIG["h"].get(k)
            SIG["g"][k] = Signal(old.sem, v, old.per * HEADS_H) if old else Signal(sem(f"att_{k}"), v)

        def ffn_signals():
            s = dict(a_pe=3, a_out=3, conv=3, gelu=1, b_pe=3, mult=3, h_hi=1, h_lo=1, prev=1, tail=2)
            sig = {k: Signal(sem(f"f_{k}"), v) for k, v in s.items()}
            sig["down"] = Signal(sem("f_down"), 2 * NT)
            sig["added"] = Signal(sem("f_added"), 2 * NT)
            return sig

        FSIG = ffn_signals()

        def ffn_sums(layer):
            return (Signal(FSIG["down"].sem, 2 * NT, layer * DOWN_ALL + 1),
                    Signal(FSIG["added"].sem, 2 * NT, layer * (DOWN_ALL - 1 + NT) + NT))

        rows_sem = sem("rows_in")
        params_rd = sem("params_ready")
        tails_pe = sem("tails_pe")
        tails_cp = sem("tails_copied")
        tails_dma = sem("tails_dma")

        def blocks(tile, m, n_tokens):
            return tile[:, 0:n_tokens].rearrange("p (g w) -> p g w", w=2 * m)

        def level_tokens(level):
            return T if level >= DEC_FROM else PROMPT

        MERGED = [("level", 0), ("vg", 0), ("vg", 1)]
        for x in range(1, NL):
            MERGED += [("level", x), ("vg", x + 1)]
        MERGED += [("vg", t) for t in range(NL + 1, NT)]

        def vg_dst(dv, t):
            return bank[6 + t % 2][:, 0:2 * dv]

        def scores(x, t):
            if t == PT:
                return bank[4 + x % 2][:, 0:P]
            return bank[2 * (x % 2) + t // 4][:, (t % 4) * P:(t % 4 + 1) * P]

        def preds_after(x):
            return 2 * (x + 1) + max(0, x - DEC_FROM + 1)

        KIND = {
            "h": dict(n="h", heads=HEADS_H, dv=DV_H, first="k", second="q", unit0=U_H, units=4, scale=1.0, w=A["hgrn_w_in"][0],
                      qc=0, kc=D, vc=2 * D, gc=3 * D, state_in=A["state_hgrn"][0], state_out=out["hgrn_p"][0, 0],
                      stream_out=out["hgrn_s"][0]),
            "g": dict(n="g", heads=HEADS_G, dv=DV_G, first="q", second="k", unit0=U_G, units=6, scale=1.0 / 16.0, w=A["gla_w_in"][0],
                      qc=0, kc=D // 2, vc=D, gc=2 * D, state_in=A["state_gla"][0], state_out=out["gla_p"][0, 0],
                      stream_out=out["gla_s"][0]),
        }
        WR = 3 * D

        def slot_count(kind, i, s):
            if kind == "h":
                per = 16 if s < 2 else 32
                return i * per + per
            base = slot_base["g"][s]
            per = 16 if s < 2 else 32
            return i * per + (base + per)

        slot_base = {}
        used = [0] * 6
        slot_base["h"] = list(used)
        for s in range(4):
            used[s] += HEADS_H * (1 if s < 2 else 2)
        slot_base["wh"] = list(used)
        for u in range(8):
            used[u % 6] += 1
        slot_base["f0"] = list(used)
        for s in range(6):
            used[s] += GROUPS
        slot_base["r"] = list(used)
        used[0] += 1
        slot_base["g"] = [16 * x for x in used]
        for s in range(6):
            used[s] += HEADS_G * (1 if s < 2 else 2)
        slot_base["wg"] = list(used)
        for u in range(8):
            used[u % 6] += 1
        slot_base["f1"] = list(used)

        block = ctx.enter_context(nc.Block())

        @block.sync
        def _(sp):
            for dst, src in ((ident, A["c_ident"]), (level_f32, A["c_level"]), (keep_f32, A["c_keep"]),
                             (own_stream, A["c_stream"]),
                             (att["h"]["norm"], A["hgrn_norm_g"][0].partition_broadcast(P))):
                sp.dma_start(dst[:], src).then_inc(const_in, 16)
            for r in range(3):
                sp.dma_start(att["h"]["lb"][:, :, r], A["lb_param"][r].rearrange("(h p) -> p h", p=P)).then_inc(const_in, 16)
            for t in range(NT):
                src = A["x_prompt"][0, t * P:(t + 1) * P, :] if t < PT else A["x_sample"].rearrange("b s d -> (b s) d")
                sp.dma_start(tm[:, t, :], src).then_inc(x_in[t], 16)

            def attention(K, i, first):
                S, w, dv, tile = SIG[K["n"]], K["w"], K["dv"], att[K["n"]]
                if not first:
                    sp.wait_ge(S["q_proj"].sem, S["q_proj"].at(i - 1, 3))
                    sp.wait_ge(S["k_proj"].sem, S["k_proj"].at(i - 1, 3))
                elif K["n"] == "g":
                    sp.wait_ge(S["r_pe"].sem, 3)
                for s, x in ((0, K["first"]), (1, K["second"])):
                    sp.dma_start(ring_raw[s][:, :].rearrange("p (k n) -> p k n", k=KD),
                                 w[:, bass.ds(i * P + K[x + "c"], P)].rearrange("(k p) n -> p k n", p=P)).then_inc(slot_in[s], 16)
                kk = UNIT // (2 * dv)
                for u in range(KD // kk):
                    if not first and u == 0:
                        sp.wait_ge(S["vg_pe"].sem, S["vg_pe"].at(i - 1, S["vg_pe"].per))
                    for part, col in ((0, K["vc"]), (1, K["gc"])):
                        dst = ring_raw[2 + u][:, :].rearrange("p (k n) -> p k n", k=kk)[:, :, part * dv:(part + 1) * dv]
                        src = w[u * kk * P:(u + 1) * kk * P, bass.ds(i * dv + col, dv)].rearrange("(k p) n -> p k n", p=P)
                        sp.dma_start(dst, src).then_inc(slot_in[2 + u], 16)
                if K["n"] == "g":
                    if not first:
                        sp.wait_ge(S["z_proj"].sem, S["z_proj"].at(i - 1, 3))
                    sp.dma_start(tile["wgk"][:, :], A["gla_w_gk2"][0][:, bass.ds(i * P, P)]).then_inc(S["wgk_in"].sem, 16)
                if not first:
                    attention_out(K, i - 1)
                    sp.wait_ge(S["stream_out"].sem, S["stream_out"].at(i - 1, 16))
                sp.dma_start(tile["s0"][:, :, :], K["state_in"][:, bass.ds(i, 1), :, :].rearrange("b o k v -> k (b o) v")
                             ).then_inc(S["s0_in"].sem, 16)

            def attention_out(K, i):
                S, tile = SIG[K["n"]], att[K["n"]]
                sp.wait_ge(S["chain"].sem, S["chain"].at(i, PT))
                sp.dma_start(K["state_out"][bass.ds(i, 1), :, :].rearrange("o k v -> k (o v)"),
                             tile["chain"][:, PT - 1, :]).then_inc(S["state_out"].sem, 16)
                sp.wait_ge(S["s0new"].sem, S["s0new"].at(i, STREAMS))
                sp.dma_start(K["stream_out"][:, bass.ds(i, 1), :, :].rearrange("b o k v -> k (b o) v"),
                             tile["s0"][:, :, :]).then_inc(S["stream_out"].sem, 16)

            def out_unit(w, u):
                half, kp = u // 4, u % 4
                sp.dma_start(ring_raw[u % 6][:, :].rearrange("p (k n) -> p k n", k=2),
                             w[kp * 2 * P:(kp + 1) * 2 * P, half * 512:(half + 1) * 512].rearrange("(k p) n -> p k n", p=P)
                             ).then_inc(slot_in[u % 6], 16)

            def out_units_first(S, w, heads):
                first, second = ("k_proj", "q_proj") if S is SIG["h"] else ("q_proj", "k_proj")
                for u, (done, cnt) in enumerate(((first, 3), (second, 3), ("vg_pe", NT))):
                    sp.wait_ge(S[done].sem, S[done].at(heads - 1, cnt))
                    out_unit(w, u)
                for u in range(3, 6):
                    out_unit(w, u)

            def out_units_last(w, layer):
                sp.wait_ge(w_done, (2 * layer + 1) * NT)
                for u in (6, 7):
                    out_unit(w, u)

            def residual_in(layer, src):
                for t in range(NT):
                    sp.wait_ge(tj_done, JOB_O[layer] + 2 * (t + 1))
                    sp.dma_start(tm[:, t, :], src(t)).then_inc(res_in[t], 16)

            def ffn_rows(layer):
                sp.dma_start(rows_in[0:2 * STREAMS, :],
                             A["state_ffn_conv"][layer].rearrange("b j f -> (b j) f")).then_inc(rows_sem, 16)
                sp.dma_start(rows_in[2 * STREAMS:2 * STREAMS + 3, :], A["ffn_conv_w"][layer]).then_inc(rows_sem, 16)
                sp.dma_start(rows_in[ROWS - 1:ROWS, :], A["ffn_conv_b"][layer:layer + 1, :]).then_inc(rows_sem, 16)

            def up_units(layer, j, waits):
                F = {k: v.layer(layer, NFF) for k, v in FSIG.items()}
                for u in range(2):
                    for part, done in ((0, "a_pe"), (1, "b_pe")):
                        if waits:
                            sp.wait_ge(F[done].sem, (j * 2 + (u - 2)) * 3 + (F[done].base + 3))
                        sp.dma_start(ring_raw[2 * u + part][:, :].rearrange("p (k n) -> p k n", k=KD),
                                     A["ffn_w_up"][layer][:, bass.ds(j * (2 * P) + (part * FF + u * P), P)]
                                     .rearrange("(k p) n -> p k n", p=P)).then_inc(slot_in[2 * u + part], 16)

            def down_units(layer, j, waits):
                if waits:
                    dn = ffn_sums(layer)[0]
                    sp.wait_ge(dn.sem, j * dn.per + dn.base)
                for u in range(2):
                    sp.dma_start(ring_raw[4 + u][:, :], A["ffn_w_down"][layer][bass.ds(j * (2 * P) + u * P, P), :]
                                 ).then_inc(slot_in[4 + u], 16)

            def lnrows(layer, kind, dst):
                for j, name in enumerate((f"ln_{kind}_g", f"ln_{kind}_b")):
                    sp.dma_start(dst[j][:, :], A[name][layer].partition_broadcast(P)).then_inc(lnrow_in, 16)

            def ffn(layer):
                state = SIG["hg"[layer]]["state_out"]
                sp.wait_ge(state.sem, state.at((HEADS_H, HEADS_G)[layer], 0))
                ffn_rows(layer)
                sp.wait_ge(w_done, (2 * layer + 2) * NT)
                up_units(layer, 0, False)
                up_units(layer, 1, True)
                down_units(layer, 0, False)
                with sp.Fori(2, GROUPS) as j:
                    up_units(layer, j, True)
                    down_units(layer, j - 1, True)
                down_units(layer, GROUPS - 1, True)
                F = FSIG["tail"].layer(layer, NFF)
                sp.wait_ge(F.sem, F.at(NFF - 1, 2))
                lnrows(layer, "ffn", ln_ffn)
                sp.wait_ge(tails_cp, 6 * (layer + 1))
                sp.dma_start(out["conv_p"][layer, 0], tails_out[0:2, :]).then_inc(tails_dma, 16)
                sp.dma_start(out["conv_s"][layer].rearrange("b j f -> (b j) f"), tails_out[2:TAILS, :]).then_inc(tails_dma, 16)

            attention(KIND["h"], 0, True)
            with sp.Fori(1, HEADS_H) as i:
                attention(KIND["h"], i, False)
            out_units_first(SIG["h"], A["hgrn_w_out"][0], HEADS_H)
            attention_out(KIND["h"], HEADS_H - 1)
            sp.wait_ge(SIG["h"]["final"].sem, SIG["h"]["final"].at(HEADS_H, 0))
            lnrows(0, "mix", ln_att)
            residual_in(0, lambda t: A["x_prompt"][0, t * P:(t + 1) * P, :] if t < PT
                        else A["x_sample"].rearrange("b s d -> (b s) d"))
            out_units_last(A["hgrn_w_out"][0], 0)
            sp.wait_ge(SIG["h"]["stream_out"].sem, SIG["h"]["stream_out"].at(HEADS_H, 0))
            ffn(0)
            sp.wait_ge(FSIG["a_pe"].sem, NFF * 3)
            sp.dma_start(ring_raw[0][:, 0:KD * RANK].rearrange("p (k n) -> p k n", k=KD),
                         A["gla_w_in"][0][:, WR:WR + RANK].rearrange("(k p) n -> p k n", p=P)).then_inc(slot_in[0], 16)
            sp.wait_ge(FSIG["down"].sem, DOWN_ALL)
            sp.wait_ge(ln_done, 2 * NT)
            sp.wait_ge(tails_dma, 32)
            for t in range(NT):
                sp.dma_start(x2_dram[t * P:(t + 1) * P, :], tm[:, t, :]).then_inc(x2_out, 16)
            sp.dma_start(att["g"]["norm"][:, :], A["gla_norm_g"][0].partition_broadcast(P)).then_inc(const_in, 16)
            sp.dma_start(att["g"]["bgk"][:, :], A["gla_b_gk2"][0].rearrange("(h p) -> p h", p=P)).then_inc(const_in, 16)
            attention(KIND["g"], 0, True)
            with sp.Fori(1, HEADS_G) as i:
                attention(KIND["g"], i, False)
            out_units_first(SIG["g"], A["gla_w_out"][0], HEADS_G)
            attention_out(KIND["g"], HEADS_G - 1)
            sp.wait_ge(SIG["g"]["final"].sem, SIG["g"]["final"].at(HEADS_G, 0))
            lnrows(1, "mix", ln_att)
            sp.wait_ge(x2_out, 16 * NT)
            residual_in(1, lambda t: x2_dram[t * P:(t + 1) * P, :])
            out_units_last(A["gla_w_out"][0], 1)
            sp.wait_ge(SIG["g"]["stream_out"].sem, SIG["g"]["stream_out"].at(HEADS_G, 0))
            ffn(1)
            for t in range(NT):
                sp.wait_ge(ln_done, 3 * NT + t + 1)
                dst = out["y_prompt"][0, t * P:(t + 1) * P, :] if t < PT else out["y_sample"].rearrange("b s d -> (b s) d")
                sp.dma_start(dst, tm[:, t, :]).then_inc(y_out, 16)
            sp.wait_ge(y_out, 16 * NT)
            sp.wait_ge(tails_dma, 64)
            for name in ("state_out", "stream_out"):
                sp.wait_ge(SIG["g"][name].sem, SIG["g"][name].at(HEADS_G, 0))

        @block.gpsimd
        def _(pool):
            pool.wait_ge(start_dve, 1)
            pool.memset(att["h"]["a"][:, :, :], 0.0)
            pool.memset(att["h"]["qz"][:, :, :], 0.0).then_inc(start_pool, 1)

            def split(unit, slot, count, width=UNIT):
                pool.wait_ge(slot_in[slot], count)
                nc.gpsimd.tensor_tensor(ring_hi[slot][:, 0:width], ring_raw[slot][:, 0:width],
                                        ones[:, :].to_broadcast([P, width]), ALU.mult).then_inc(unit_hi, 1)
                pool.wait_ge(unit_hi, unit + 1)
                nc.gpsimd.tensor_tensor(ring_lo[slot][:, 0:width], ring_raw[slot][:, 0:width],
                                        ring_hi[slot][:, 0:width].bitcast(F32), ALU.subtract).then_inc(unit_split, 1)

            def head_units(K, i):
                for s in range(K["units"]):
                    split(i * K["units"] + (K["unit0"] + s), s, slot_count(K["n"], i, s))

            def out_units(base, unit0):
                for u in range(8):
                    split(unit0 + u, u % 6, 16 * (base[u % 6] + 1 + u // 6))

            def ffn_units(base, unit0):
                def up(j, unit):
                    for s in range(4):
                        split(unit + s, s, (j + 1) * 16 + 16 * base[s])

                def down(j, unit):
                    for s in range(2):
                        split(unit + s, 4 + s, (j + 1) * 16 + 16 * base[4 + s])

                up(0, unit0)
                with pool.Fori(1, GROUPS) as j:
                    up(j, j * 6 + (unit0 - 2))
                    down(j - 1, j * 6 + (unit0 + 2))
                down(GROUPS - 1, unit0 + 6 * GROUPS - 2)

            with pool.Fori(0, HEADS_H) as i:
                head_units(KIND["h"], i)
            out_units(slot_base["wh"], U_WH)
            ffn_units(slot_base["f0"], U_F0)
            split(U_R, 0, 16 * (slot_base["r"][0] + 1), KD * RANK)
            pool.wait_ge(FSIG["down"].sem, DOWN_ALL)
            pool.wait_ge(ln_done, 2 * NT)
            pool.wait_ge(tails_dma, 32)
            pool.memset(att["g"]["a"][:, :, :], 0.0)
            pool.memset(att["g"]["qz"][:, :, :], 0.0).then_inc(start_pool, 1)
            with pool.Fori(0, HEADS_G) as i:
                head_units(KIND["g"], i)
            out_units(slot_base["wg"], U_WG)
            ffn_units(slot_base["f1"], U_F1)

        @block.tensor
        def _(pe):
            def mm3(dst, w_hi, w_lo, x_hi, x_lo, start, stop):
                nc.tensor.matmul(dst, w_hi, x_hi, start=start, stop=False)
                nc.tensor.matmul(dst, w_hi, x_lo, start=False, stop=False)
                return nc.tensor.matmul(dst, w_lo, x_hi, start=False, stop=stop)

            def project_feature_major(slot, b0, done, width=P, before=None):
                for c in range(NC):
                    if before:
                        before(c)
                    for k in range(KD):
                        last = mm3(bank[b0 + c][0:width, 0:CH],
                                   ring_hi[slot][:, k * width:(k + 1) * width], ring_lo[slot][:, k * width:(k + 1) * width],
                                   xt_hi[:, k, c * CH:(c + 1) * CH], xt_lo[:, k, c * CH:(c + 1) * CH],
                                   k == 0, k == KD - 1)
                    last.then_inc(done, 1)

            def transpose_tile(t, job):
                for hf in range(2):
                    if job + hf >= 2:
                        pe.wait_ge(tj_lo, job + hf - 1)
                    for k in range(4):
                        kk = 4 * hf + k
                        last = nc.tensor.transpose(bank[4 + hf][:, k * P:(k + 1) * P], tm[:, t, kk * P:(kk + 1) * P], ident[:, :])
                    last.then_inc(tj_done, 1)

            def attention(K, i, first, last_):
                n, dv = K["n"], K["dv"]
                S, tile = SIG[n], att[n]
                U = i * K["units"] + K["unit0"]
                npj = S["kvp_pe"].per

                def wait(name, it, k):
                    pe.wait_ge(S[name].sem, S[name].at(it, k))

                if not last_:
                    pe.wait_ge(unit_split, U + 1)
                    if not first:
                        wait("pred", i - 1, S["pred"].per)

                    def chunk_ready(c):
                        pe.wait_ge(tj_lo, 2 * TPC * (c + 1))
                    project_feature_major(0, 0, S[K["first"] + "_proj"].sem, before=(chunk_ready if first and n == "h" else None))
                if not first:
                    p = i - 1
                    wait("kh", p, 1)
                    wait("vg", p, NT)
                    if last_:
                        wait("pred", p, S["pred"].per)
                    for jb, (b, tiles) in enumerate(((6, range(0, 4)), (3, range(4, 8)), (4, range(8, 9)))):
                        for x, t in enumerate(tiles):
                            last = nc.tensor.transpose(bank[b][:, x * P:(x + 1) * P], tile["c0"][:, t * P:(t + 1) * P], ident[:, :])
                        last.then_inc(S["kt_pe"].sem, 1)
                    for t in range(NT):
                        last = nc.tensor.matmul(bank[7][:, t:t + 1], tile["c1"][:, t * P:(t + 1) * P], ones[:, :],
                                                start=True, stop=True)
                    last.then_inc(S["dots_pe"].sem, 1)
                    wait("kt", p, 3)
                    per_job = 512 // dv
                    for jb, b in zip(range(npj), (5, 6, 3, 4)):
                        for x in range(per_job):
                            c = jb * per_job + x
                            last = nc.tensor.matmul(bank[b][:, x * dv:(x + 1) * dv], tile["kt"][:, c, :], tile["v"][:, c, :],
                                                    start=True, stop=True)
                        last.then_inc(S["kvp_pe"].sem, 1)
                    wait("dots", p, 1)
                    wait("qz", p, 1)
                    pe.wait_ge(S["s0_in"].sem, S["s0_in"].at(p, 16))
                    nc.tensor.matmul(bank[7][:, 0:dv], tile["a"][:, PT, :], tile["v"][:, PT, :], start=True, stop=False)
                    for s in range(STREAMS):
                        last = nc.tensor.matmul(bank[7][:, 0:dv], tile["qz"][:, s, :], tile["s0"][:, s, :],
                                                start=False, stop=(s == STREAMS - 1))
                    last.then_inc(S["odec_pe"].sem, 1)
                    wait("vz", p, 1)
                    for jb, b in zip(range(npj), (3, 4) if n == "h" else (5, 6, 3, 4)):
                        if n == "g":
                            wait("chain", p, (jb + 1) * per_job)
                        last = nc.tensor.matmul(bank[b][:, :], tile["kt"][:, PT, :],
                                                tile["vz"][:, :, :].rearrange("p s v -> p (s v)")[:, jb * 512:(jb + 1) * 512],
                                                start=True, stop=True)
                        last.then_inc(S["kvd_pe"].sem, 1)
                if n == "g" and not last_:
                    pe.wait_ge(S["wgk_in"].sem, S["wgk_in"].at(i, 16))
                    pe.wait_ge(S["rt"].sem, 3)
                    for c in range(NC):
                        wait("q_ready", i, c + 1)
                        nc.tensor.matmul(bank[c][:, 0:CH].rearrange("p (t n) -> p t n", n=P), tile["wgk"][:, :],
                                         rt[:, c * TPC:(c + 1) * TPC, :], start=True, stop=True).then_inc(S["z_proj"].sem, 1)
                if not last_:
                    pe.wait_ge(unit_split, U + 2)
                    if not first:
                        wait("s0new", i - 1, STREAMS)
                        wait("chain", i - 1, PT)
                    project_feature_major(1, 3, S[K["second"] + "_proj"].sem)
                if not first:
                    p = i - 1
                    wait("chain", p, PT)
                    wait("qh", p, 1)
                    wait("o_add", p, 1)
                    if n == "g":
                        wait("s0new", p, STREAMS)
                    for jb in range(npj):
                        if jb >= 2:
                            wait("o_add", p, 1 + (jb - 1) * per_job)
                        for x in range(per_job):
                            c = jb * per_job + x
                            dst = bank[6 + jb % 2][:, x * dv:(x + 1) * dv]
                            last = nc.tensor.matmul(dst, tile["a"][:, c, :], tile["v"][:, c, :], start=True, stop=(c == 0))
                            if c > 0:
                                last = nc.tensor.matmul(dst, tile["qh"][:, c * P:(c + 1) * P], tile["chain"][:, c - 1, :],
                                                        start=False, stop=True)
                        last.then_inc(S["o_pe"].sem, 1)
                if not last_:
                    kk = UNIT // (2 * dv)
                    for what, x in MERGED:
                        if what == "vg":
                            if x == 0:
                                pe.wait_ge(unit_split, U + K["units"])
                            if x < 2 and not first:
                                wait("o_add", i - 1, NT if x else NT - 512 // dv)
                            if x >= 2:
                                wait("vg", i, x - 1)
                            dst = vg_dst(dv, x)
                            for k in range(KD):
                                s, c = 2 + k // kk, (k % kk) * 2 * dv
                                xh, xl = xt_hi[:, k, x * P:(x + 1) * P], xt_lo[:, k, x * P:(x + 1) * P]
                                last = mm3(dst, xh, xl, ring_hi[s][:, c:c + 2 * dv], ring_lo[s][:, c:c + 2 * dv],
                                           k == 0, k == KD - 1)
                            last.then_inc(S["vg_pe"].sem, 1)
                        else:
                            c = tile["c0"] if x % 2 == 0 else tile["c1"]
                            if x == 0:
                                wait("k_sig" if n == "h" else "k_ready", i, 3 if n == "h" else 1)
                                wait("q_ready" if n == "h" else "z_min", i, 3)
                            wait("lvl", i, x + 1)
                            if x >= 2:
                                wait("pred", i, preds_after(x - 2))
                            for t in range(PT + (1 if x >= DEC_FROM else 0)):
                                ct = c[:, t * P:(t + 1) * P]
                                last = nc.tensor.matmul(scores(x, t), ct, ct, start=True, stop=True)
                            last.then_inc(S["lvl_pe"].sem, 1)

            def out_projection(layer, unit0, job0):
                S, heads = (SIG["h"], HEADS_H) if layer == 0 else (SIG["g"], HEADS_G)
                pe.wait_ge(S["final"].sem, S["final"].at(heads, 0))
                for t in range(NT):
                    transpose_tile(t, job0 + 2 * t)
                job = job0 + 2 * NT
                for half in range(2):
                    pe.wait_ge(unit_split, unit0 + 4 * (half + 1))
                    for t in range(NT):
                        n = (2 * layer + half) * NT + t
                        if half == 0:
                            pe.wait_ge(tj_lo, job0 + 2 * (t + 1))
                        if n >= 2:
                            pe.wait_ge(w_added, n - 1)
                        for k in range(KD):
                            s = (4 * half + k // 2) % 6
                            c = (k % 2) * 512
                            last = mm3(bank[6 + n % 2][:, :], xt_hi[:, k, t * P:(t + 1) * P], xt_lo[:, k, t * P:(t + 1) * P],
                                       ring_hi[s][:, c:c + 512], ring_lo[s][:, c:c + 512], k == 0, k == KD - 1)
                        last.then_inc(w_done, 1)
                        if half == 1 and t >= 2:
                            pe.wait_ge(ln_done, 2 * layer * NT + t - 1)
                            transpose_tile(t - 2, job + 2 * (t - 2))
                for t in (NT - 2, NT - 1):
                    pe.wait_ge(ln_done, 2 * layer * NT + t + 1)
                    transpose_tile(t, job + 2 * t)

            def ffn(layer, unit0, job0, job_next):
                F = {k: v.layer(layer, NFF) for k, v in FSIG.items()}
                DN, AD = ffn_sums(layer)

                pe.wait_ge(rows_sem, 48 * (layer + 1))
                pe.wait_ge(w_added, (2 * layer + 2) * NT)
                for f in range(NFF):
                    last = nc.tensor.transpose(bank[3][:, f * ROWS:(f + 1) * ROWS], rows_in[:, f * P:(f + 1) * P],
                                               ident[0:ROWS, 0:ROWS])
                last.then_inc(DN.sem, 1)

                def up(j, unit, first=False):
                    for u in range(2):
                        f = j * 2 + u
                        pe.wait_ge(unit_split, unit + (2 * u + 1))
                        pe.wait_ge(F["a_out"].sem, F["a_out"].at(f, 0))

                        def ready(c):
                            if first and u == 0:
                                pe.wait_ge(tj_lo, job0 + 2 * TPC * (c + 1))
                        project_feature_major(2 * u, 0, F["a_pe"].sem, before=ready)
                        pe.wait_ge(unit_split, unit + (2 * u + 2))
                        if first and u == 0:
                            pe.wait_ge(params_rd, layer + 1)
                        pe.wait_ge(F["mult"].sem, F["mult"].at(f, 0))
                        project_feature_major(2 * u + 1, 3, F["b_pe"].sem)

                def down(j, g, unit, after_tile=None):
                    pe.wait_ge(unit_split, unit + 2)
                    pe.wait_ge(F["h_lo"].sem, F["h_lo"].at(j * 2 + 1, 1))
                    for t in range(NT):
                        for n in range(2):
                            pe.wait_ge(AD.sem, AD.at(j, max(0, 2 * t + n - 1)))
                            for u in range(2):
                                last = mm3(bank[6 + n][:, :], h_hi[g][u][:, t * P:(t + 1) * P], h_lo[g][u][:, t * P:(t + 1) * P],
                                           ring_hi[4 + u][:, n * 512:(n + 1) * 512], ring_lo[4 + u][:, n * 512:(n + 1) * 512],
                                           u == 0, u == 1)
                            last.then_inc(DN.sem, 1)
                        if after_tile:
                            after_tile(t)

                up(0, unit0, True)
                with pe.Fori(0, GROUPS // 2) as pair:
                    j = pair * 2 + 1
                    up(j, j * 6 + (unit0 - 2))
                    down(j - 1, 0, j * 6 + (unit0 + 2))
                    up(j + 1, j * 6 + (unit0 + 4))
                    down(j, 1, j * 6 + (unit0 + 8))
                pe.wait_ge(F["tail"].sem, F["tail"].at(NFF - 1, 2))
                pe.wait_ge(F["a_out"].sem, F["a_out"].at(NFF - 1, 3))
                for b in range(6):
                    if b >= 3:
                        pe.wait_ge(tails_cp, 6 * layer + b - 2)
                    for x in range(4 if b < 5 else 2):
                        f = 4 * b + x
                        last = nc.tensor.transpose(bank[b % 3][0:TAILS, x * P:(x + 1) * P], tails[:, f, :], ident[:, :])
                    last.then_inc(tails_pe, 1)

                def after_tile(t):
                    if layer == 0 and t >= 2:
                        pe.wait_ge(ln_done, (2 * layer + 1) * NT + t - 1)
                        transpose_tile(t - 2, job_next + 2 * (t - 2))

                pe.wait_ge(F["mult"].sem, F["mult"].at(NFF - 1, 3))
                down(GROUPS - 1, 0, unit0 + 6 * GROUPS - 2, after_tile)
                if layer == 0:
                    for t in (NT - 2, NT - 1):
                        pe.wait_ge(ln_done, (2 * layer + 1) * NT + t + 1)
                        transpose_tile(t, job_next + 2 * t)

            pe.wait_ge(const_in, 16 * 8)
            for t in range(NT):
                pe.wait_ge(x_in[t], 16)
                transpose_tile(t, 2 * t)
            pe.wait_ge(start_pool, 1)
            pe.wait_ge(start_dve, 1)
            attention(KIND["h"], 0, True, False)
            with pe.Fori(1, HEADS_H) as i:
                attention(KIND["h"], i, False, False)
            attention(KIND["h"], HEADS_H, False, True)
            out_projection(0, U_WH, JOB_O[0])
            ffn(0, U_F0, JOB_F[0], JOB_G)
            pe.wait_ge(unit_split, U_R + 1)
            pe.wait_ge(tails_cp, 6)

            def r_ready(c):
                pe.wait_ge(tj_lo, JOB_G + 2 * TPC * (c + 1))
            project_feature_major(0, 0, SIG["g"]["r_pe"].sem, width=RANK, before=r_ready)
            pe.wait_ge(start_pool, 2)
            pe.wait_ge(SIG["g"]["rt"].sem, 3)
            attention(KIND["g"], 0, True, False)
            with pe.Fori(1, HEADS_G) as i:
                attention(KIND["g"], i, False, False)
            attention(KIND["g"], HEADS_G, False, True)
            out_projection(1, U_WG, JOB_O[1])
            ffn(1, U_F1, JOB_F[1], None)

        @block.scalar
        def _(act):
            def activate(*a, **k):
                return nc.scalar.activation(*a, **k)

            def take_transposed(t, job):
                for hf in range(2):
                    act.wait_ge(tj_done, job + hf + 1)
                    activate(xt_hi[:, 4 * hf:4 * hf + 4, t * P:(t + 1) * P],
                             bank[4 + hf][:, :].rearrange("p (k n) -> p k n", k=4), ACT.Copy).then_inc(tj_hi, 1)

            def ln_rstd(t, n):
                act.wait_ge(ln_moments, n + 1)
                activate(log_var[:, t:t + 1], moments[:, t, 1:2], ACT.Ln, bias=eps_ln[:, :]).then_inc(ln_log, 1)
                act.wait_ge(ln_log, n + 1)
                activate(inv_std[:, t:t + 1], log_var[:, t:t + 1], ACT.Exp, scale=-0.5).then_inc(ln_std, 1)

            def attention(K, i, first, last_):
                n, dv = K["n"], K["dv"]
                S, tile = SIG[n], att[n]

                def wait(name, it, k):
                    act.wait_ge(S[name].sem, S[name].at(it, k))

                def cols(c):
                    return slice(c * CH, (c + 1) * CH)

                def token_keys():
                    p = i - 1
                    for jb, (b, t0, t1) in enumerate(((6, 0, 4), (3, 4, 8), (4, 8, 9))):
                        wait("kt_pe", p, jb + 1)
                        activate(tile["kt"][:, t0:t1, :], bank[b][:, 0:(t1 - t0) * P].rearrange("p (t n) -> p t n", n=P),
                                 ACT.Copy).then_inc(S["kt"].sem, 1)

                def level(x):
                    m, c = LEVELS[x], tile["c0"] if x % 2 == 0 else tile["c1"]
                    v = blocks(c, m, level_tokens(x))
                    wait("sub", i, x + 1)
                    activate(v[:, :, 0:m], v[:, :, 0:m], ACT.Exp, scale=-K["scale"])
                    activate(v[:, :, m:2 * m], v[:, :, m:2 * m], ACT.Exp, scale=K["scale"]).then_inc(S["exp"].sem, 1)

                def squares():
                    p = i - 1
                    for x, t in enumerate([PT] + list(range(PT))):
                        wait("o_add", p, x + 1)
                        if x > 0:
                            wait("squares", p, x)
                        activate(tile["junk"][:, :], tile["v"][:, t, :], ACT.Square, accum_out=tile["ss"][:, t:t + 1]
                                 ).then_inc(S["squares"].sem, 1)

                def rms():
                    p = i - 1
                    wait("squares", p, NT)
                    activate(tile["lss"][:, :], tile["ss"][:, :], ACT.Ln, scale=1.0 / dv, bias=eps_rms[:, :]).then_inc(S["lss"].sem, 1)
                    wait("lss", p, 1)
                    activate(tile["rstd"][:, :], tile["lss"][:, :], ACT.Exp, scale=-0.5).then_inc(S["rstd"].sem, 1)

                def take_vg(t):
                    wait("vg_pe", i, t + 1)
                    if t == 0 and not first:
                        wait("gated_o", i - 1, 1)
                        wait("squares", i - 1, NT)
                    src = vg_dst(dv, t)
                    activate(tile["v"][:, t, :], src[:, 0:dv], ACT.Copy)
                    activate(tm[:, t, bass.ds(i * dv, dv)], src[:, dv:2 * dv], ACT.Copy).then_inc(S["vg"].sem, 1)

                if not first:
                    wait("vg", i - 1, NT)
                    g = tm[:, :, bass.ds((i - 1) * dv, dv)]
                    if n == "h":
                        activate(tile["gt"][:, :, :], g, ACT.Sigmoid).then_inc(S["g_act"].sem, 1)
                    else:
                        activate(g, g, ACT.Silu).then_inc(S["g_act"].sem, 1)
                if n == "h":
                    if not first:
                        token_keys()
                    if not last_:
                        if not first:
                            wait("kvd_pe", i - 1, S["kvd_pe"].per)
                        for c in range(NC):
                            wait("k_proj", i, c + 1)
                            activate(tile["c1"][:, cols(c)], bank[c][:, 0:CH], ACT.Sigmoid).then_inc(S["k_sig"].sem, 1)
                        wait("forget", i, 1)
                        activate(tile["c0"][:, :], tile["c1"][:, :], ACT.Ln).then_inc(S["log_f"].sem, 1)
                        level(0)
                        for c in range(NC):
                            wait("q_proj", i, c + 1)
                            activate(tile["q"][:, cols(c)], bank[3 + c][:, 0:CH], ACT.Sigmoid).then_inc(S["q_sig"].sem, 1)
                else:
                    if not last_:
                        if not first:
                            wait("qh", i - 1, 1)
                        for c in range(NC):
                            wait("q_proj", i, c + 1)
                            activate(tile["q"][:, cols(c)], bank[c][:, 0:CH], ACT.Copy, scale=float(P) ** -0.5
                                     ).then_inc(S["q_ready"].sem, 1)
                        activate(tile["bcol"][:, :], tile["bgk"][:, bass.ds(i, 1)], ACT.Copy).then_inc(S["bcol"].sem, 1)
                    if not first:
                        token_keys()
                    if not last_:
                        if not first:
                            wait("kvd_pe", i - 1, S["kvd_pe"].per)
                        wait("bcol", i, 1)
                        for c in range(NC):
                            wait("z_proj", i, c + 1)
                            activate(tile["c0"][:, cols(c)], bank[c][:, 0:CH], ACT.Abs, bias=tile["bcol"][:, :]
                                     ).then_inc(S["z_abs"].sem, 1)
                        wait("z_abs", i, 3)
                        activate(tile["c0"][:, :], tile["c0"][:, :], ACT.Exp, scale=-1.0).then_inc(S["z_exp"].sem, 1)
                        wait("z_exp", i, 1)
                        activate(tile["c0"][:, :], tile["c0"][:, :], ACT.Ln, bias=ones[:, :]).then_inc(S["z_log"].sem, 1)
                        level(0)
                        for c in range(NC):
                            wait("k_proj", i, c + 1)
                            last = activate(tile["k"][:, cols(c)], bank[3 + c][:, 0:CH], ACT.Copy)
                        last.then_inc(S["k_ready"].sem, 1)
                if not first:
                    squares()
                if last_:
                    rms()
                    return
                for t in range(NL - 1):
                    level(t + 1)
                    if t == 0 and not first:
                        rms()
                    take_vg(t)
                if not first:
                    wait("o_add", i - 1, NT)
                    act.wait_ge(S["state_out"].sem, S["state_out"].at(i - 1, 16))
                activate(tile["e"][:, :], tile["b"][:, :], ACT.Exp, scale=K["scale"]).then_inc(S["e"].sem, 1)
                take_vg(NL - 1)
                wait("kh_sub", i, 2)
                activate(tile["c0"][:, :], tile["c0"][:, :], ACT.Exp, scale=-K["scale"]).then_inc(S["kh_exp"].sem, 1)
                for t in range(NL, NT):
                    take_vg(t)

            def out_projection(layer, job0):
                for t in range(NT):
                    take_transposed(t, job0 + 2 * t)
                job = job0 + 2 * NT
                for t in range(NT + 2):
                    if t < NT:
                        ln_rstd(t, 2 * layer * NT + t)
                    if t >= 2:
                        act.wait_ge(w_done, (2 * layer + 1) * NT + t - 1)
                        take_transposed(t - 2, job + 2 * (t - 2))

            def ffn(layer, job_next):
                F = {k: v.layer(layer, NFF) for k, v in FSIG.items()}
                DN, _ = ffn_sums(layer)

                def wait(name, f, k):
                    act.wait_ge(F[name].sem, F[name].at(f, k))

                def tile(j, u, g, first=False):
                    f = j * 2 + u
                    for c in range(NC):
                        wait("a_pe", f, c + 1)
                        if c == 0 and not first:
                            wait("tail", f - 2, 2)
                        n = min(PROMPT, (c + 1) * CH) - c * CH
                        last = activate(ax[u][:, 2 + c * CH:2 + c * CH + n], bank[c][:, 0:n], ACT.Copy)
                        if n < CH:
                            dst = ax[u][:, 2 + PROMPT:].rearrange("p (s w) -> p s w", s=STREAMS)[:, :, 2:]
                            last = activate(dst, bank[c][:, n:CH].rearrange("p (s w) -> p s w", s=STREAMS), ACT.Copy)
                        last.then_inc(F["a_out"].sem, 1)
                    wait("conv", f, 3)
                    activate(cv[u][:, :], cv[u][:, :], ACT.Gelu_apprx_tanh).then_inc(F["gelu"].sem, 1)
                    wait("mult", f, 3)
                    if not first:
                        act.wait_ge(DN.sem, DN.at(j - 1, 0))
                    activate(h_hi[g][u][:, :], cv[u][:, :], ACT.Copy).then_inc(F["h_hi"].sem, 1)

                tile(0, 0, 0, True)
                tile(0, 1, 0, True)
                with act.Fori(0, GROUPS // 2) as pair:
                    j = pair * 2 + 1
                    for u in range(2):
                        tile(j, u, 1)
                    for u in range(2):
                        tile(j + 1, u, 0)
                for b in range(6):
                    act.wait_ge(tails_pe, 6 * layer + b + 1)
                    if b == 0:
                        act.wait_ge(DN.sem, DN.at(GROUPS - 1, 0))
                    w = 512 if b < 5 else 256
                    activate(tails_out[:, b * 512:b * 512 + w], bank[b % 3][0:TAILS, 0:w], ACT.Copy).then_inc(tails_cp, 1)
                for t in range(NT + 2):
                    if t < NT:
                        ln_rstd(t, (2 * layer + 1) * NT + t)
                    if t >= 2 and job_next is not None:
                        take_transposed(t - 2, job_next + 2 * (t - 2))

            act.wait_ge(start_dve, 1)
            for t in range(NT):
                take_transposed(t, 2 * t)
            act.wait_ge(prep, 2)
            activate(att["h"]["lbx"][:, :, :], att["h"]["lbx"][:, :, :], ACT.Exp).then_inc(prep, 1)
            attention(KIND["h"], 0, True, False)
            with act.Fori(1, HEADS_H) as i:
                attention(KIND["h"], i, False, False)
            attention(KIND["h"], HEADS_H, False, True)
            out_projection(0, JOB_O[0])
            ffn(0, JOB_G)
            for c in range(NC):
                act.wait_ge(SIG["g"]["r_pe"].sem, c + 1)
                if c == 0:
                    act.wait_ge(x2_out, 16 * NT)
                activate(rt[:, c * TPC:(c + 1) * TPC, :], bank[c][0:RANK, 0:CH].rearrange("p (t n) -> p t n", n=P),
                         ACT.Copy).then_inc(SIG["g"]["rt"].sem, 1)
            act.wait_ge(const_in, 16 * 10)
            attention(KIND["g"], 0, True, False)
            with act.Fori(1, HEADS_G) as i:
                attention(KIND["g"], i, False, False)
            attention(KIND["g"], HEADS_G, False, True)
            out_projection(1, JOB_O[1])
            ffn(1, None)

        @block.vector
        def _(dve):
            V = nc.vector

            def take_transposed(t, job):
                for hf in range(2):
                    dve.wait_ge(tj_hi, job + hf + 1)
                    V.tensor_tensor(xt_lo[:, 4 * hf:4 * hf + 4, t * P:(t + 1) * P],
                                    bank[4 + hf][:, :].rearrange("p (k n) -> p k n", k=4),
                                    xt_hi[:, 4 * hf:4 * hf + 4, t * P:(t + 1) * P].bitcast(F32), ALU.subtract).then_inc(tj_lo, 1)

            def ln_stats(t, n):
                for hf in range(2):
                    last = V.bn_stats(stats[:, t % 2, hf, :], tm[:, t, hf * 512:(hf + 1) * 512])
                last.then_inc(ln_step, 1)
                dve.wait_ge(ln_step, n + 1)
                V.bn_aggr(moments[:, t, :], stats[:, t % 2, :, :]).then_inc(ln_moments, 1)

            def ln_apply(t, n, rows):
                dve.wait_ge(ln_std, n + 1)
                V.tensor_scalar(tm[:, t, :], tm[:, t, :], moments[:, t, 0:1], inv_std[:, t:t + 1],
                                ALU.subtract, ALU.mult).then_inc(ln_a, 1)
                dve.wait_ge(ln_a, 2 * n + 1)
                V.tensor_tensor(tm[:, t, :], tm[:, t, :], rows[0][:, :], ALU.mult).then_inc(ln_a, 1)
                dve.wait_ge(ln_a, 2 * n + 2)
                V.tensor_tensor(tm[:, t, :], tm[:, t, :], rows[1][:, :], ALU.add).then_inc(ln_done, 1)

            def attention(K, i, first, last_):
                n, dv = K["n"], K["dv"]
                S, tile = SIG[n], att[n]

                def wait(name, it, k):
                    dve.wait_ge(S[name].sem, S[name].at(it, k))

                def cols(c):
                    return slice(c * CH, (c + 1) * CH)

                if not first:
                    p = i - 1
                    gate(K, p)
                    wait("dots_pe", p, 1)
                    V.tensor_copy(tile["dot"][:, :], bank[7][:, 0:NT]).then_inc(S["dots"].sem, 1)
                    chain_tail(K, p)
                if not last_:
                    if n == "h":
                        wait("k_sig", i, 3)
                        V.tensor_scalar(tile["c1"][:, :], tile["c1"][:, :], tile["span"][:, bass.ds(i, 1), 0],
                                        tile["floor"][:, bass.ds(i, 1), 0], ALU.mult, ALU.add).then_inc(S["forget"].sem, 1)
                        wait("forget", i, 1)
                        V.tensor_scalar(tile["k"][:, :], tile["c1"][:, :], -1.0, 1.0, ALU.mult, ALU.add).then_inc(S["forget"].sem, 1)
                        wait("log_f", i, 1)
                        src = tile["c0"]
                    else:
                        for c in range(NC):
                            wait("z_abs", i, c + 1)
                            V.tensor_scalar(tile["c1"][:, cols(c)], bank[c][:, 0:CH], tile["bcol"][:, :], 0.0,
                                            ALU.add, ALU.min).then_inc(S["z_min"].sem, 1)
                        wait("z_min", i, 3)
                        wait("z_log", i, 1)
                        V.tensor_tensor(tile["c1"][:, :], tile["c1"][:, :], tile["c0"][:, :], ALU.subtract
                                        ).then_inc(S["scan_in"].sem, 1)
                        wait("scan_in", i, 1)
                        src = tile["c1"]
                    V.tensor_tensor_scan(tile["b"][:, :], keep[:, :], src[:, :], 0.0, ALU.mult, ALU.add).then_inc(S["scanned"].sem, 1)
                    wait("scanned", i, 1)

                    def sub(x):
                        m, c = LEVELS[x], tile["c0"] if x % 2 == 0 else tile["c1"]
                        if x >= 2:
                            wait("lvl_pe", i, x - 1)
                            if x >= 3:
                                wait("pred", i, preds_after(x - 3))
                        b = blocks(tile["b"], m, level_tokens(x))
                        V.tensor_tensor(blocks(c, m, level_tokens(x)), b, b[:, :, m - 1:m].to_broadcast([P, b.shape[1], 2 * m]),
                                        ALU.subtract).then_inc(S["sub"].sem, 1)

                    def decay(x):
                        m, c = LEVELS[x], tile["c0"] if x % 2 == 0 else tile["c1"]
                        v = blocks(c, m, level_tokens(x))
                        if x == 0:
                            if n == "g":
                                wait("k_ready", i, 1)
                            else:
                                wait("q_ready", i, 3)
                        wait("exp", i, x + 1)
                        V.tensor_tensor(v[:, :, 0:m], v[:, :, 0:m], blocks(tile["k"], m, level_tokens(x))[:, :, 0:m], ALU.mult)
                        V.tensor_tensor(v[:, :, m:2 * m], v[:, :, m:2 * m], blocks(tile["q"], m, level_tokens(x))[:, :, m:2 * m],
                                        ALU.mult).then_inc(S["lvl"].sem, 1)

                    def place_scores(x):
                        m = LEVELS[x]
                        mask = level_mask[:, x * 64:(x + 1) * 64].rearrange("p (g w) -> p g w", w=m)
                        parts = [(0, 4, bank[2 * (x % 2)]), (4, 8, bank[2 * (x % 2) + 1])]
                        if x >= DEC_FROM:
                            parts.append((PT, NT, bank[4 + x % 2]))
                        for t0, t1, ps in parts:
                            nt = t1 - t0
                            dst = tile["a"][:, t0:t1, :].rearrange("p t (g w) -> p t g w", w=2 * m)[:, :, :, m:2 * m]
                            src = ps[:, 0:nt * P].rearrange("p (t g w) -> p t g w", t=nt, w=2 * m)[:, :, :, m:2 * m]
                            msk = mask.unsqueeze(1).to_broadcast([P, nt, 64 // m, m])
                            V.copy_predicated(dst, msk, src).then_inc(S["pred"].sem, 1)

                    sub(0)
                    if n == "h":
                        for c in range(NC):
                            wait("q_sig", i, c + 1)
                            V.tensor_tensor(tile["q"][:, cols(c)], bank[3 + c][:, 0:CH], tile["q"][:, cols(c)], ALU.mult
                                            ).then_inc(S["q_ready"].sem, 1)
                    decay(0)
                if not first:
                    add_diagonal(K, i - 1)
                if not last_:
                    sub(1)
                if not first:
                    apply_gate(K, i - 1)
                if not last_:
                    decay(1)
                if not first:
                    apply_rms(K, i - 1)
                if last_:
                    return
                for x in range(2, NL):
                    sub(x)
                    place_scores(x - 2)
                    decay(x)
                wait("lvl_pe", i, NL - 1)
                wait("pred", i, preds_after(NL - 3))
                V.tensor_tensor(tile["c1"][:, :], tile["q"][:, :], tile["k"][:, :], ALU.mult).then_inc(S["prod"].sem, 1)
                place_scores(NL - 2)
                wait("lvl_pe", i, NL)
                wait("pred", i, preds_after(NL - 2))
                bp = tile["b"][:, 0:PROMPT].rearrange("p (t n) -> p t n", n=P)
                bs = tile["b"][:, PROMPT:T].rearrange("p (s n) -> p s n", n=STREAM_T)
                V.tensor_tensor(tile["c0"][:, PROMPT:T].rearrange("p (s n) -> p s n", n=STREAM_T), bs,
                                bs[:, :, STREAM_T - 1:STREAM_T].to_broadcast([P, STREAMS, STREAM_T]), ALU.subtract
                                ).then_inc(S["kh_sub"].sem, 1)
                place_scores(NL - 1)
                V.tensor_tensor(tile["c0"][:, 0:PROMPT].rearrange("p (t n) -> p t n", n=P), bp,
                                bp[:, :, P - 1:P].to_broadcast([P, PT, P]), ALU.subtract).then_inc(S["kh_sub"].sem, 1)
                wait("e", i, 1)
                V.tensor_tensor(tile["qh"][:, :], tile["q"][:, :], tile["e"][:, :], ALU.mult).then_inc(S["qh"].sem, 1)
                V.tensor_copy(tile["dec"][:, 0:PT], tile["e"][:, 0:PROMPT].rearrange("p (t n) -> p t n", n=P)[:, :, P - 1])
                V.tensor_copy(tile["dec"][:, PT:PT + STREAMS],
                              tile["e"][:, PROMPT:T].rearrange("p (s n) -> p s n", n=STREAM_T)[:, :, STREAM_T - 1]
                              ).then_inc(S["dec"].sem, 1)
                wait("qh", i, 1)
                for s in range(STREAMS):
                    last = V.tensor_copy(tile["qz"][:, s, s * STREAM_T:(s + 1) * STREAM_T],
                                         tile["qh"][:, PROMPT + s * STREAM_T:PROMPT + (s + 1) * STREAM_T])
                last.then_inc(S["qz"].sem, 1)
                wait("kh_exp", i, 1)
                V.tensor_tensor(tile["c0"][:, :], tile["c0"][:, :], tile["k"][:, :], ALU.mult).then_inc(S["kh"].sem, 1)

            def chain_tail(K, p):
                n, dv = K["n"], K["dv"]
                S, tile = SIG[n], att[n]
                per_job = 512 // dv

                def wait(name, it, k):
                    dve.wait_ge(S[name].sem, S[name].at(it, k))

                wait("kt_pe", p, 3)
                v8 = tile["v"][:, PT, :].unsqueeze(1).to_broadcast([P, STREAMS, dv])
                own = own_stream[:, :].unsqueeze(2).to_broadcast([P, STREAMS, dv])
                V.tensor_tensor(tile["vz"][:, :, :], v8, own, ALU.mult).then_inc(S["vz"].sem, 1)
                for c in range(PT):
                    jb, x = c // per_job, c % per_job
                    kv = bank[(5, 6, 3, 4)[jb]][:, x * dv:(x + 1) * dv]
                    if x == 0:
                        wait("kvp_pe", p, jb + 1)
                    if c == 0:
                        wait("dec", p, 1)
                        V.tensor_copy(tile["chain"][:, 0, :], kv).then_inc(S["chain"].sem, 1)
                    else:
                        wait("chain", p, c)
                        V.scalar_tensor_tensor(tile["chain"][:, c, :], tile["chain"][:, c - 1, :], tile["dec"][:, c:c + 1], kv,
                                               ALU.mult, ALU.add).then_inc(S["chain"].sem, 1)
                wait("odec_pe", p, 1)
                V.scalar_tensor_tensor(tile["v"][:, PT, :], tile["v"][:, PT, :], tile["dot"][:, PT:NT], bank[7][:, 0:dv],
                                       ALU.mult, ALU.add).then_inc(S["o_add"].sem, 1)
                for s in range(STREAMS):
                    jb, x = s // per_job, s % per_job
                    kv = bank[((3, 4) if n == "h" else (5, 6, 3, 4))[jb]][:, x * dv:(x + 1) * dv]
                    if x == 0:
                        wait("kvd_pe", p, jb + 1)
                    V.scalar_tensor_tensor(tile["s0"][:, s, :], tile["s0"][:, s, :], tile["dec"][:, PT + s:PT + s + 1], kv,
                                           ALU.mult, ALU.add).then_inc(S["s0new"].sem, 1)

            def add_diagonal(K, p):
                n, dv = K["n"], K["dv"]
                S, tile = SIG[n], att[n]
                per_job = 512 // dv
                for c in range(PT):
                    jb, x = c // per_job, c % per_job
                    if x == 0:
                        dve.wait_ge(S["o_pe"].sem, S["o_pe"].at(p, jb + 1))
                    V.scalar_tensor_tensor(tile["v"][:, c, :], tile["v"][:, c, :], tile["dot"][:, c:c + 1],
                                           bank[6 + jb % 2][:, x * dv:(x + 1) * dv], ALU.mult, ALU.add).then_inc(S["o_add"].sem, 1)

            def gate(K, p):
                n, dv = K["n"], K["dv"]
                S, tile = SIG[n], att[n]
                g = tm[:, :, bass.ds(p * dv, dv)]
                dve.wait_ge(S["g_act"].sem, S["g_act"].at(p, 1))
                if n == "h":
                    V.tensor_tensor(g, g, tile["gt"][:, :, :], ALU.mult).then_inc(S["gated"].sem, 1)
                    dve.wait_ge(S["gated"].sem, S["gated"].at(p, 1))
                V.tensor_tensor(g, g, tile["norm"][:, :].unsqueeze(1).to_broadcast([P, NT, dv]), ALU.mult).then_inc(S["gated"].sem, 1)

            def apply_gate(K, p):
                dv, S, tile = K["dv"], SIG[K["n"]], att[K["n"]]
                g = tm[:, :, bass.ds(p * dv, dv)]
                dve.wait_ge(S["gated"].sem, S["gated"].at(p, S["gated"].per))
                dve.wait_ge(S["o_add"].sem, S["o_add"].at(p, NT))
                V.tensor_tensor(g, g, tile["v"][:, :, :], ALU.mult).then_inc(S["gated_o"].sem, 1)

            def apply_rms(K, p):
                dv, S, tile = K["dv"], SIG[K["n"]], att[K["n"]]
                g = tm[:, :, bass.ds(p * dv, dv)]
                dve.wait_ge(S["gated_o"].sem, S["gated_o"].at(p, 1))
                dve.wait_ge(S["rstd"].sem, S["rstd"].at(p, 1))
                V.tensor_tensor(g, g, tile["rstd"][:, :].unsqueeze(2).to_broadcast([P, NT, dv]), ALU.mult
                                ).then_inc(S["final"].sem, 1)

            def out_projection(layer, job0):
                for t in range(NT):
                    take_transposed(t, job0 + 2 * t)
                job = job0 + 2 * NT
                dve.wait_ge(lnrow_in, 32 * (2 * layer + 1))
                for half in range(2):
                    for t in range(NT + (2 if half else 0)):
                        if t < NT:
                            if half == 0:
                                dve.wait_ge(res_in[t], 16 * (layer + 1))
                            m = (2 * layer + half) * NT + t
                            dve.wait_ge(w_done, m + 1)
                            x = tm[:, t, half * 512:(half + 1) * 512]
                            V.scalar_tensor_tensor(x, x, ALPHA, bank[6 + m % 2][:, :], ALU.mult, ALU.add).then_inc(w_added, 1)
                            if half == 1:
                                dve.wait_ge(w_added, m + 1)
                                ln_stats(t, 2 * layer * NT + t)
                        if half == 1 and 1 <= t <= NT:
                            ln_apply(t - 1, 2 * layer * NT + t - 1, ln_att)
                        if half == 1 and t >= 2:
                            take_transposed(t - 2, job + 2 * (t - 2))
                            scale_residual(t - 2, layer)

            def scale_residual(t, layer):
                V.tensor_scalar(tm[:, t, :], tm[:, t, :], ALPHA, None, ALU.mult).then_inc(FSIG["added"].sem, 1)

            def ffn(layer, job_next):
                F = {k: v.layer(layer, NFF) for k, v in FSIG.items()}
                DN, AD = ffn_sums(layer)

                def wait(name, f, k):
                    dve.wait_ge(F[name].sem, F[name].at(f, k))

                dve.wait_ge(DN.sem, DN.at(0, 0))
                V.tensor_copy(params[:, :, :], bank[3][:, 0:NFF * ROWS].rearrange("p (f r) -> p f r", r=ROWS)).then_inc(params_rd, 1)
                for u in range(2):
                    V.memset(ax[u][:, 0:2], 0.0)
                dve.wait_ge(params_rd, layer + 1)

                def param(f, r):
                    return params[:, bass.ds(f, 1), 2 * STREAMS + r]

                def conv(f, u):
                    dec = ax[u][:, 2 + PROMPT:].rearrange("p (s w) -> p s w", s=STREAMS)
                    V.tensor_copy(dec[:, :, 0:2], params[:, bass.ds(f, 1), 0:2 * STREAMS].rearrange("p o (s w) -> p (o s) w", s=STREAMS)
                                  ).then_inc(F["prev"].sem, 1)
                    wait("a_out", f, 3)
                    wait("prev", f, 1)
                    parts = [(cv[u][:, 0:PROMPT], lambda j: ax[u][:, j:j + PROMPT]),
                             (cv[u][:, PROMPT:T].rearrange("p (s w) -> p s w", s=STREAMS), lambda j: dec[:, :, j:j + STREAM_T])]
                    for j in range(3):
                        for x, (dst, tap) in enumerate(parts):
                            if j == 0:
                                ins = V.tensor_scalar(dst, tap(0), param(f, 0), param(f, 3), ALU.mult, ALU.add)
                            else:
                                ins = V.scalar_tensor_tensor(dst, tap(j), param(f, j), dst, ALU.mult, ALU.add)
                            if x == 1:
                                ins.then_inc(F["conv"].sem, 1)
                        if j < 2:
                            wait("conv", f, j + 1)

                def keep_tail(f, u):
                    dec = ax[u][:, 2 + PROMPT:].rearrange("p (s w) -> p s w", s=STREAMS)
                    V.tensor_copy(tails[:, bass.ds(f, 1), 0:2], ax[u][:, PROMPT:PROMPT + 2].unsqueeze(1)).then_inc(F["tail"].sem, 1)
                    V.tensor_copy(tails[:, bass.ds(f, 1), 2:TAILS].rearrange("p o (s w) -> p (o s) w", s=STREAMS),
                                  dec[:, :, STREAM_T:STREAM_T + 2]).then_inc(F["tail"].sem, 1)

                def multiply(f, u):
                    wait("gelu", f, 1)
                    for c in range(NC):
                        wait("b_pe", f, c + 1)
                        x = cv[u][:, c * CH:(c + 1) * CH]
                        V.tensor_tensor(x, x, bank[3 + c][:, 0:CH], ALU.mult).then_inc(F["mult"].sem, 1)

                def split(f, u, g):
                    wait("h_hi", f, 1)
                    V.tensor_tensor(h_lo[g][u][:, :], cv[u][:, :], h_hi[g][u][:, :].bitcast(F32), ALU.subtract
                                    ).then_inc(F["h_lo"].sem, 1)

                def add_down(j, t):
                    for n in range(2):
                        dve.wait_ge(DN.sem, DN.at(j, 2 * t + n + 1))
                        x = tm[:, t, n * 512:(n + 1) * 512]
                        V.tensor_tensor(x, x, bank[6 + n][:, :], ALU.add).then_inc(AD.sem, 1)

                def group(j, g, down):
                    for u in range(2):
                        f = j * 2 + u
                        conv(f, u)
                        keep_tail(f, u)
                        multiply(f, u)
                        if u == 0:
                            split(f, u, g)
                    if down:
                        for t in range(NT):
                            if t == 0:
                                dve.wait_ge(AD.sem, AD.at(j - 1, 0))
                            add_down(j - 1, t)
                    split(j * 2 + 1, 1, g)

                group(0, 0, False)
                with dve.Fori(0, GROUPS // 2) as pair:
                    j = pair * 2 + 1
                    group(j, 1, True)
                    group(j + 1, 0, True)
                dve.wait_ge(AD.sem, AD.at(GROUPS - 1, 0))
                dve.wait_ge(lnrow_in, 32 * (2 * layer + 2))
                n0 = (2 * layer + 1) * NT
                for t in range(NT + 2):
                    if t < NT:
                        add_down(GROUPS - 1, t)
                        dve.wait_ge(AD.sem, AD.at(GROUPS - 1, 2 * t + 2))
                        ln_stats(t, n0 + t)
                    if 1 <= t <= NT:
                        ln_apply(t - 1, n0 + t - 1, ln_ffn)
                    if t >= 2 and job_next is not None:
                        take_transposed(t - 2, job_next + 2 * (t - 2))

            V.memset(ones[:, :], 1.0)
            V.memset(eps_ln[:, :], LN_EPS)
            V.memset(eps_rms[:, :], RMS_EPS).then_inc(start_dve, 1)
            dve.wait_ge(const_in, 16 * 8)
            V.tensor_copy(level_mask[:, :], level_f32[:, :])
            V.tensor_copy(keep[:, :], keep_f32[:, :])
            h = att["h"]
            V.reduce_max(h["lbs"][:, :, :], h["lb"][:, :, :], AX.X).then_inc(prep, 1)
            dve.wait_ge(prep, 1)
            V.tensor_tensor(h["lbx"][:, :, :], h["lb"][:, :, :], h["lbs"][:, :, :].to_broadcast([P, HEADS_H, 3]), ALU.subtract
                            ).then_inc(prep, 1)
            for t in range(NT):
                take_transposed(t, 2 * t)
            dve.wait_ge(prep, 3)
            V.reduce_sum(h["lbs"][:, :, :], h["lbx"][:, :, :], AX.X).then_inc(prep, 1)
            dve.wait_ge(prep, 4)
            V.reciprocal(h["span"][:, :, :], h["lbs"][:, :, :]).then_inc(prep, 1)
            dve.wait_ge(prep, 5)
            V.tensor_tensor(h["floor"][:, :, :], h["span"][:, :, :], h["lbx"][:, :, 0:1], ALU.mult).then_inc(prep, 1)
            dve.wait_ge(prep, 6)
            V.tensor_scalar(h["span"][:, :, :], h["floor"][:, :, :], -1.0, 1.0, ALU.mult, ALU.add).then_inc(prep, 1)
            dve.wait_ge(prep, 7)
            dve.wait_ge(start_pool, 1)
            attention(KIND["h"], 0, True, False)
            with dve.Fori(1, HEADS_H) as i:
                attention(KIND["h"], i, False, False)
            attention(KIND["h"], HEADS_H, False, True)
            out_projection(0, JOB_O[0])
            ffn(0, JOB_G)
            dve.wait_ge(const_in, 16 * 10)
            dve.wait_ge(start_pool, 2)
            attention(KIND["g"], 0, True, False)
            with dve.Fori(1, HEADS_G) as i:
                attention(KIND["g"], i, False, False)
            attention(KIND["g"], HEADS_G, False, True)
            out_projection(1, JOB_O[1])
            ffn(1, None)


_INS = ["x_prompt", "x_sample", "state_hgrn", "state_gla", "state_ffn_conv", "lb_param", "hgrn_w_in", "hgrn_w_out",
        "hgrn_norm_g", "gla_w_in", "gla_w_gk2", "gla_b_gk2", "gla_w_out", "gla_norm_g", "ln_mix_g", "ln_mix_b",
        "ffn_w_up", "ffn_conv_w", "ffn_conv_b", "ffn_w_down", "ln_ffn_g", "ln_ffn_b"]
_OUTS = [("y_prompt", (1, PROMPT, D)), ("y_sample", (STREAMS, STREAM_T, D)),
         ("hgrn_p", (1, 1, HEADS_H, P, DV_H)), ("hgrn_s", (1, STREAMS, HEADS_H, P, DV_H)),
         ("gla_p", (1, 1, HEADS_G, P, DV_G)), ("gla_s", (1, STREAMS, HEADS_G, P, DV_G)),
         ("conv_p", (2, 1, 2, FF)), ("conv_s", (2, STREAMS, 2, FF))]


def kernel(**inputs):
    import numpy as _np
    import concourse.bacc as _bacc
    from concourse import mybir as _mybir
    from concourse.bass_utils import run_bass_kernel_spmd as _run

    key = _np.arange(P)[:, None]
    level = _np.zeros((P, NL * 64), _np.float32)
    for x, m in enumerate(LEVELS):
        block_of_query = _np.arange(64)[None, :] // m
        level[:, x * 64:(x + 1) * 64] = (key // (2 * m) == block_of_query) & (key % (2 * m) < m)
    keep = _np.ones((P, T), _np.float32)
    keep[:, 0:PROMPT:P] = 0
    keep[:, PROMPT:T:STREAM_T] = 0
    consts = {
        "c_ident": _np.eye(P, dtype=_np.float32), "c_level": level, "c_keep": keep,
        "c_stream": (key // STREAM_T == _np.arange(STREAMS)[None, :]).astype(_np.float32),
    }

    nc = _bacc.Bacc("TRN2", target_bir_lowering=False, num_devices=1, dynamic_dma_scratch_size=1024)
    arrays, ins, outs = {}, {}, {}
    for name in _INS:
        arrays[f"in_{name}"] = _np.ascontiguousarray(inputs[name])
        ins[name] = nc.dram_tensor(f"in_{name}", arrays[f"in_{name}"].shape, _mybir.dt.float32, kind="ExternalInput").ap()
    for name, a in consts.items():
        arrays[f"in_{name}"] = a
        ins[name] = nc.dram_tensor(f"in_{name}", a.shape, _mybir.dt.from_np(a.dtype), kind="ExternalInput").ap()
    for name, shape in _OUTS:
        outs[name] = nc.dram_tensor(f"out_{name}", shape, _mybir.dt.float32, kind="ExternalOutput").ap()
    build(nc, ins, outs)
    r = _run(nc, [arrays], core_ids=[0])
    return tuple(r.results[0][f"out_{name}"] for name, _ in _OUTS)
```

```python
import concourse.bass as bass
from concourse import mybir
from contextlib import ExitStack

P = 128
D = 1024
KD = D // P
PROMPT, STREAMS, STREAM_T = 1024, 8, 16
T = PROMPT + STREAMS * STREAM_T
NT = T // P
PT = PROMPT // P
CH = 384
NC = T // CH
TPC = CH // P
FF = 2816
NFF = FF // P
GROUPS = NFF // 2
DOWN_ALL = (GROUPS - 1) * 2 * NT + 1
W_SLOTS = [4, 5, 2, 3, 6, 7, 8, 9]
DOWN_SLOTS, DOWN_SLOTS_LAST = (4, 5), (1, 2)
R_SLOT = 3
SLOTS = 10

O_AHEAD = [[2, 3], []] + [[_t + 2] for _t in range(2, NT - 2)] + [[], []]
W_ORDER = [("o", 0), ("o", 1)]
for _t in range(NT):
    W_ORDER += [("o", _x) for _x in O_AHEAD[_t]] + ([("n", _t - 1)] if _t >= 1 else [])
W_ORDER.append(("n", NT - 1))
HEADS_H, HEADS_G = 8, 4
DV_H, DV_G = 128, 256
RANK = 16
ALPHA = 4.0 ** 0.25
LN_EPS, RMS_EPS = 1e-5, 1e-6
LEVELS = [64, 32, 16, 8, 4, 2, 1]
NL = len(LEVELS)
DEC_FROM = LEVELS.index(STREAM_T // 2)
UNIT = 1024
ROWS = 2 * STREAMS + 4
TAILS = 2 + 2 * STREAMS

JOB_O = (2 * NT, 8 * NT)
JOB_G = 6 * NT

U_H = 0
U_WH = U_H + 4 * HEADS_H
U_F0 = U_WH + 8
U_R = U_F0 + 6 * GROUPS
U_G = U_R + 1
U_WG = U_G + 6 * HEADS_G
U_F1 = U_WG + 8


def w_job(layer, kind, t):
    return JOB_O[layer] + 2 * W_ORDER.index((kind, t))


class Signal:

    def __init__(self, sem, per, base=0):
        self.sem, self.per, self.base = sem, per, base

    def at(self, i, k):
        return i * self.per + (self.base + k)

    def layer(self, n, passes):
        return Signal(self.sem, self.per, n * self.per * passes)


def build(nc, A, out):
    F32, F32R, U8 = mybir.dt.float32, mybir.dt.float32r, mybir.dt.uint8
    ALU, ACT = mybir.AluOpType, mybir.ActivationFunctionType
    AX = mybir.AxisListType

    with ExitStack() as ctx:
        ctx.enter_context(nc.allow_non_contiguous_dma(reason="small parameters"))

        cursor = [1152]

        def place(name, shape, dt, offset=None):
            size = (4 if dt != U8 else 1)
            for s in shape[1:]:
                size *= s
            size = -(-size // 32) * 32
            if offset is None:
                offset = cursor[0]
                cursor[0] += size
            return nc.alloc_sbuf_tensor_at(name, shape, dt, offset=offset)

        ident = place("ident", [P, P], F32)
        level_mask = place("level_mask", [P, NL * 64], U8)
        keep = place("keep", [P, T], U8)
        own_stream = place("own_stream", [P, STREAMS], F32)
        ones = place("ones", [P, 1], F32)
        eps_ln = place("eps_ln", [P, 1], F32)
        eps_rms = place("eps_rms", [P, 1], F32)
        stats = place("stats", [P, 2, 2, 6], F32)
        moments = place("moments", [P, NT, 2], F32)
        std = place("std", [P, NT], F32)
        neg_mean = place("neg_mean", [P, NT], F32)
        inv_std = place("inv_std", [P, NT], F32)

        xt_hi = place("xt_hi", [P, KD, T], F32R)
        xt_lo_at = cursor[0]
        xt_lo = place("xt_lo", [P, KD, T], F32R)
        tm = place("tm", [P, NT, D], F32)
        ring_hi, ring_lo, ring_raw = [], [], []
        for s in range(SLOTS):
            if s == 6:
                work = cursor[0]
            ring_hi.append(place(f"ring_hi{s}", [P, UNIT], F32R))
            at = cursor[0]
            ring_lo.append(place(f"ring_lo{s}", [P, UNIT], F32R))
            ring_raw.append(place(f"ring_raw{s}", [P, UNIT], F32, at))
        ln_att = [place(f"ln_att{j}", [P, D], F32) for j in range(2)]
        rows_in = place("rows_in", [ROWS, FF], F32)
        rows_at = cursor[0] - FF * 4

        att = {}

        def attention_tiles(n, dv):
            cursor[0] = work
            t = {}
            for name in ("q", "qh", "k", "b", "c0", "c1"):
                t[name] = place(f"{n}_{name}", [P, T], F32)
            kt_at = work + 2 * T * 4
            t["kt"] = place(f"{n}_kt", [P, NT, P], F32, kt_at)
            t["vz"] = place(f"{n}_vz", [P, STREAMS, dv], F32, work + 4 * T * 4)
            t["a"] = place(f"{n}_a", [P, NT, P], F32)
            t["v"] = place(f"{n}_v", [P, NT, dv], F32)
            at = cursor[0]
            t["chain"] = place(f"{n}_chain", [P, PT, dv], F32)
            t["e"] = place(f"{n}_e", [P, T], F32, at)
            cursor[0] = max(cursor[0], at + T * 4)
            t["s0"] = place(f"{n}_s0", [P, STREAMS, dv], F32)
            t["qz"] = place(f"{n}_qz", [P, STREAMS, P], F32)
            if n == "h":
                t["gt"] = place("h_gt", [P, NT, dv], F32)
                t["lb"] = place("h_lb", [P, HEADS_H, 3], F32)
                t["lbx"] = place("h_lbx", [P, HEADS_H, 3], F32)
                t["lbs"] = place("h_lbs", [P, HEADS_H, 1], F32)
                t["floor"] = place("h_floor", [P, HEADS_H, 1], F32)
                t["span"] = place("h_span", [P, HEADS_H, 1], F32)
            else:
                t["wgk"] = place("g_wgk", [RANK, P], F32)
                t["bgk"] = place("g_bgk", [P, HEADS_G], F32)
                t["bcol"] = place("g_bcol", [P, 1], F32)
            t["norm"] = place(f"{n}_norm", [P, dv], F32)
            t["junk"] = place(f"{n}_junk", [P, dv], F32)
            t["dec"] = place(f"{n}_dec", [P, 2 * STREAMS], F32)
            t["dot"] = place(f"{n}_dot", [P, NT], F32)
            t["ss"] = place(f"{n}_ss", [P, NT], F32)
            t["rms"] = place(f"{n}_rms", [P, NT], F32)
            t["rstd"] = place(f"{n}_rstd", [P, NT], F32)
            assert cursor[0] <= nc.sbuf_usable_end, (n, cursor[0])
            att[n] = t

        attention_tiles("h", DV_H)
        attention_tiles("g", DV_G)
        rt = tm[0:RANK, :, D - P:D]

        level_f32 = place("level_f32", [P, NL * 64], F32, work)
        keep_f32 = place("keep_f32", [P, T], F32, work + T * 4)

        cursor[0] = work
        h_hi, h_lo = [], []
        for g in range(2):
            h_hi.append([place(f"h_hi{g}{u}", [P, T], F32R) for u in range(2)])
            h_lo.append([place(f"h_lo{g}{u}", [P, T], F32R) for u in range(2)])
        tails_out = place("tails_out", [TAILS, FF], F32, xt_lo_at)
        ax_at = cursor[0]
        assert ax_at <= rows_at
        ax = [place(f"ax{u}", [P, 2 + PROMPT + STREAMS * (2 + STREAM_T)], F32) for u in range(2)]
        cv = [place(f"cv{u}", [P, T], F32) for u in range(2)]
        params = place("params", [P, NFF, ROWS], F32)
        tails = place("tails", [P, NFF, TAILS], F32)
        assert cursor[0] <= nc.sbuf_usable_end, cursor[0]
        ln_ffn = [place(f"ln_ffn{j}", [P, D], F32, ax_at + j * D * 4) for j in range(2)]

        bank = [ctx.enter_context(nc.psum_tensor(f"bank{i}", [P, 512], F32)) for i in range(8)]
        x2_dram = nc.dram_tensor("x2_scratch", (T, D), F32, kind="Internal").ap()

        def sem(name):
            return ctx.enter_context(nc.semaphore(name))

        ident_in = sem("ident_in")
        const_in = sem("const_in")
        x_in = [sem(f"x_in{t}") for t in range(NT)]
        slot_in = [sem(f"slot_in{s}") for s in range(SLOTS)]
        unit_hi = sem("unit_hi")
        w_hi = sem("w_hi")
        unit_split = sem("unit_split")
        tj_done = sem("tj_done")
        tj_hi = sem("tj_hi")
        tj_lo = sem("tj_lo")
        w_done = sem("w_done")
        w_added = sem("w_added")
        ln_moments = sem("ln_moments")
        ln_sqrt = sem("ln_sqrt")
        ln_neg = sem("ln_neg")
        ln_centered = sem("ln_centered")
        ln_scaled = sem("ln_scaled")
        ln_std = sem("ln_std")
        ln_step = sem("ln_step")
        ln_a = sem("ln_apply")
        ln_done = sem("ln_done")
        res_io = [sem(f"res_io{t}") for t in range(NT)]
        y_out = sem("y_out")
        lnrow_in = sem("lnrow_in")
        prep = sem("prep")
        start_dve = sem("start_dve")
        start_pool = sem("start_pool")

        def attention_signals(n, dv):
            npj = PT * dv // 512
            s = dict(
                q_proj=3, k_proj=3, z_proj=3, q_sig=3, k_sig=3, q_ready=3, k_ready=1, g_act=1,
                log_f=1, z_abs=3, z_min=3, z_exp=1, z_log=1, scan_in=1, scanned=1,
                sub=NL, exp=NL, lvl=NL, lvl_pe=NL, pred=2 * NL + NL - DEC_FROM, e=1, dec=1, prod=1, qh=1, qz=1, kh_sub=2, kh_exp=1,
                kh=1, kt_pe=3, kt=3, dots_pe=1, dots=1, vz=1, kvp_pe=npj, chain=PT, odec_pe=1,
                kvd_pe=npj, s0new=STREAMS, o_pe=npj, o_add=NT, squares=NT, rms=1, rstd=1, gated_o=1, final=1,
                gated=2 if n == "h" else 1, vg_pe=NT, vg=NT, forget=2,
            )
            s.update(s0_in=16, state_out=16, stream_out=16)
            only = dict(h=("q_sig", "k_sig", "log_f", "forget"),
                        g=("z_proj", "z_abs", "z_min", "z_exp", "z_log", "scan_in", "k_ready"))
            s = {k: v for k, v in s.items() if k not in only["g" if n == "h" else "h"]}
            if n == "g":
                s.update(wgk_in=16, r_pe=3, rt=3, bcol=1)
            return s

        SIG = {"h": {k: Signal(sem(f"att_{k}"), v) for k, v in attention_signals("h", DV_H).items()}, "g": {}}
        for k, v in attention_signals("g", DV_G).items():
            old = SIG["h"].get(k)
            SIG["g"][k] = Signal(old.sem, v, old.per * HEADS_H) if old else Signal(sem(f"att_{k}"), v)

        def ffn_signals():
            s = dict(a_pe=3, a_out=3, conv=3, gelu=1, b_pe=3, mult=3, h_hi=1, h_lo=1, prev=1, tail=2)
            sig = {k: Signal(sem(f"f_{k}"), v) for k, v in s.items()}
            sig["down"] = Signal(sem("f_down"), 2 * NT)
            sig["added"] = Signal(sem("f_added"), 2 * NT)
            return sig

        FSIG = ffn_signals()

        def ffn_sums(layer):
            return (Signal(FSIG["down"].sem, 2 * NT, layer * DOWN_ALL + 1),
                    Signal(FSIG["added"].sem, 2 * NT, layer * (DOWN_ALL - 1 + NT) + NT))

        rows_sem = sem("rows_in")
        params_rd = sem("params_ready")
        tails_pe = sem("tails_pe")
        tails_cp = sem("tails_copied")
        tails_dma = sem("tails_dma")

        def blocks(tile, m, n_tokens):
            return tile[:, 0:n_tokens].rearrange("p (g w) -> p g w", w=2 * m)

        def level_tokens(level):
            return T if level >= DEC_FROM else PROMPT

        SECOND_BANKS = (5, 3, 4)

        MERGED = [("level", 0), ("vg", 0), ("vg", 1)]
        for x in range(1, NL):
            MERGED += [("level", x), ("vg", x + 1)]
        MERGED += [("vg", t) for t in range(NL + 1, NT)]

        def vg_dst(dv, t):
            return bank[6 + t % 2][:, 0:2 * dv]

        def scores(x, t):
            if t == PT:
                return bank[4 + x % 2][:, 0:P]
            return bank[2 * (x % 2) + t // 4][:, (t % 4) * P:(t % 4 + 1) * P]

        def preds_after(x):
            return 2 * (x + 1) + max(0, x - DEC_FROM + 1)

        KIND = {
            "h": dict(n="h", heads=HEADS_H, dv=DV_H, first="k", second="q", unit0=U_H, units=4, scale=1.0, w=A["hgrn_w_in"][0],
                      qc=0, kc=D, vc=2 * D, gc=3 * D, state_in=A["state_hgrn"][0], state_out=out["hgrn_p"][0, 0],
                      stream_out=out["hgrn_s"][0]),
            "g": dict(n="g", heads=HEADS_G, dv=DV_G, first="q", second="k", unit0=U_G, units=6, scale=1.0 / 16.0, w=A["gla_w_in"][0],
                      qc=0, kc=D // 2, vc=D, gc=2 * D, state_in=A["state_gla"][0], state_out=out["gla_p"][0, 0],
                      stream_out=out["gla_s"][0]),
        }
        WR = 3 * D

        def slot_count(kind, i, s):
            if kind == "h":
                per = 16 if s < 2 else 32
                return i * per + per
            base = slot_base["g"][s]
            per = 16 if s < 2 else 32
            return i * per + (base + per)

        slot_base = {}
        used = [0] * SLOTS
        slot_base["h"] = list(used)
        for s in range(4):
            used[s] += HEADS_H * (1 if s < 2 else 2)
        slot_base["wh"] = list(used)
        for slot in W_SLOTS:
            used[slot] += 1
        slot_base["f0"] = list(used)

        def ffn_uses():
            for slot in range(6):
                used[slot] += GROUPS - (slot in DOWN_SLOTS)
            for slot in DOWN_SLOTS_LAST:
                used[slot] += 1

        ffn_uses()
        slot_base["r"] = list(used)
        used[R_SLOT] += 1
        slot_base["g"] = [16 * x for x in used]
        for s in range(6):
            used[s] += HEADS_G * (1 if s < 2 else 2)
        slot_base["wg"] = list(used)
        for slot in W_SLOTS:
            used[slot] += 1
        slot_base["f1"] = list(used)

        block = ctx.enter_context(nc.Block())

        @block.sync
        def _(sp):
            sp.dma_start(ident[:], A["c_ident"]).then_inc(ident_in, 16)

            def first_unit(slot, col):
                sp.dma_start(ring_raw[slot][:, :].rearrange("p (k n) -> p k n", k=KD),
                             A["hgrn_w_in"][0][:, col:col + P].rearrange("(k p) n -> p k n", p=P)).then_inc(slot_in[slot], 16)

            first_unit(0, D)
            for t in range(NT):
                src = A["x_prompt"][0, t * P:(t + 1) * P, :] if t < PT else A["x_sample"].rearrange("b s d -> (b s) d")
                sp.dma_start(tm[:, t, :], src).then_inc(x_in[t], 16)
                if t == TPC - 1:
                    first_unit(1, 0)
            for dst, src in ((level_f32, A["c_level"]), (keep_f32, A["c_keep"]),
                             (own_stream, A["c_stream"]),
                             (att["h"]["norm"], A["hgrn_norm_g"][0].partition_broadcast(P))):
                sp.dma_start(dst[:], src).then_inc(const_in, 16)
            for r in range(3):
                sp.dma_start(att["h"]["lb"][:, :, r], A["lb_param"][r].rearrange("(h p) -> p h", p=P)).then_inc(const_in, 16)

            def attention(K, i, first):
                S, w, dv, tile = SIG[K["n"]], K["w"], K["dv"], att[K["n"]]
                if not first:
                    sp.wait_ge(S["q_proj"].sem, S["q_proj"].at(i - 1, 3))
                    sp.wait_ge(S["k_proj"].sem, S["k_proj"].at(i - 1, 3))
                for s, x in () if first else ((0, K["first"]), (1, K["second"])):
                    sp.dma_start(ring_raw[s][:, :].rearrange("p (k n) -> p k n", k=KD),
                                 w[:, bass.ds(i * P + K[x + "c"], P)].rearrange("(k p) n -> p k n", p=P)).then_inc(slot_in[s], 16)
                kk = UNIT // (2 * dv)
                if first and K["n"] == "g":
                    sp.wait_ge(S["r_pe"].sem, 3)
                for u in range(KD // kk):
                    if not first and u == 0:
                        sp.wait_ge(S["vg_pe"].sem, S["vg_pe"].at(i - 1, S["vg_pe"].per))
                    for part, col in ((0, K["vc"]), (1, K["gc"])):
                        dst = ring_raw[2 + u][:, :].rearrange("p (k n) -> p k n", k=kk)[:, :, part * dv:(part + 1) * dv]
                        src = w[u * kk * P:(u + 1) * kk * P, bass.ds(i * dv + col, dv)].rearrange("(k p) n -> p k n", p=P)
                        sp.dma_start(dst, src).then_inc(slot_in[2 + u], 16)
                if K["n"] == "g" and not first:
                    sp.wait_ge(S["z_proj"].sem, S["z_proj"].at(i - 1, 3))
                    sp.dma_start(tile["wgk"][:, :], A["gla_w_gk2"][0][:, bass.ds(i * P, P)]).then_inc(S["wgk_in"].sem, 16)
                if not first:
                    attention_out(K, i - 1)
                    sp.wait_ge(S["stream_out"].sem, S["stream_out"].at(i - 1, 16))
                sp.dma_start(tile["s0"][:, :, :], K["state_in"][:, bass.ds(i, 1), :, :].rearrange("b o k v -> k (b o) v")
                             ).then_inc(S["s0_in"].sem, 16)

            def attention_out(K, i):
                S, tile = SIG[K["n"]], att[K["n"]]
                sp.wait_ge(S["chain"].sem, S["chain"].at(i, PT))
                sp.dma_start(K["state_out"][bass.ds(i, 1), :, :].rearrange("o k v -> k (o v)"),
                             tile["chain"][:, PT - 1, :]).then_inc(S["state_out"].sem, 16)
                sp.wait_ge(S["s0new"].sem, S["s0new"].at(i, STREAMS))
                sp.dma_start(K["stream_out"][:, bass.ds(i, 1), :, :].rearrange("b o k v -> k (b o) v"),
                             tile["s0"][:, :, :]).then_inc(S["stream_out"].sem, 16)

            def out_unit(w, u):
                half, kp = u // 4, u % 4
                sp.dma_start(ring_raw[W_SLOTS[u]][:, :].rearrange("p (k n) -> p k n", k=2),
                             w[kp * 2 * P:(kp + 1) * 2 * P, half * 512:(half + 1) * 512].rearrange("(k p) n -> p k n", p=P)
                             ).then_inc(slot_in[W_SLOTS[u]], 16)

            def out_units(K, w):
                S, heads = SIG[K["n"]], K["heads"]
                for u in range(4):
                    if u == (2 if K["n"] == "h" else 0):
                        sp.wait_ge(S["vg_pe"].sem, S["vg_pe"].at(heads - 1, NT))
                    out_unit(w, u)
                attention_out(K, heads - 1)
                sp.wait_ge(S["o_pe"].sem, S["o_pe"].at(heads, 0))
                for u in range(4, 7):
                    out_unit(w, u)
                sp.wait_ge(S["final"].sem, S["final"].at(heads, 0))
                out_unit(w, 7)

            def residual_in(layer, src):
                for t in range(NT):
                    sp.wait_ge(tj_done, w_job(layer, "o", t) + 2)
                    sp.dma_start(tm[:, t, :], src(t)).then_inc(res_io[t], 16)

            def before_ffn(K, layer, src):
                S = SIG[K["n"]]
                up_units(layer, 0, False, (0,))
                for name in ("state_out", "stream_out"):
                    sp.wait_ge(S[name].sem, S[name].at(K["heads"], 0))
                lnrows(layer, "mix", ln_att)
                ffn_rows(layer)
                residual_in(layer, src)

            def ffn_rows(layer):
                sp.dma_start(rows_in[0:2 * STREAMS, :],
                             A["state_ffn_conv"][layer].rearrange("b j f -> (b j) f")).then_inc(rows_sem, 16)
                sp.dma_start(rows_in[2 * STREAMS:2 * STREAMS + 3, :], A["ffn_conv_w"][layer]).then_inc(rows_sem, 16)
                sp.dma_start(rows_in[ROWS - 1:ROWS, :], A["ffn_conv_b"][layer:layer + 1, :]).then_inc(rows_sem, 16)

            def up_units(layer, j, waits, tiles=(0, 1)):
                F = {k: v.layer(layer, NFF) for k, v in FSIG.items()}
                for u in tiles:
                    for part, done in ((0, "a_pe"), (1, "b_pe")):
                        if waits:
                            sp.wait_ge(F[done].sem, (j * 2 + (u - 2)) * 3 + (F[done].base + 3))
                        sp.dma_start(ring_raw[2 * u + part][:, :].rearrange("p (k n) -> p k n", k=KD),
                                     A["ffn_w_up"][layer][:, bass.ds(j * (2 * P) + (part * FF + u * P), P)]
                                     .rearrange("(k p) n -> p k n", p=P)).then_inc(slot_in[2 * u + part], 16)

            def down_units(layer, j, waits, slots=DOWN_SLOTS):
                if waits:
                    dn = ffn_sums(layer)[0]
                    sp.wait_ge(dn.sem, j * dn.per + dn.base)
                for u in range(2):
                    sp.dma_start(ring_raw[slots[u]][:, :], A["ffn_w_down"][layer][bass.ds(j * (2 * P) + u * P, P), :]
                                 ).then_inc(slot_in[slots[u]], 16)

            def lnrows(layer, kind, dst):
                for j, name in enumerate((f"ln_{kind}_g", f"ln_{kind}_b")):
                    sp.dma_start(dst[j][:, :], A[name][layer].partition_broadcast(P)).then_inc(lnrow_in, 16)

            def ffn(layer):
                sp.wait_ge(w_done, (2 * layer + 2) * NT)
                up_units(layer, 0, False, (1,))
                up_units(layer, 1, True)
                down_units(layer, 0, False)
                with sp.Fori(2, GROUPS) as j:
                    up_units(layer, j, True)
                    down_units(layer, j - 1, True)
                F = {k: v.layer(layer, NFF) for k, v in FSIG.items()}
                sp.wait_ge(F["a_pe"].sem, F["a_pe"].at(NFF - 1, 3))
                down_units(layer, GROUPS - 1, False, DOWN_SLOTS_LAST)
                if layer == 0:
                    sp.dma_start(ring_raw[0][:, :].rearrange("p (k n) -> p k n", k=KD),
                                 A["gla_w_in"][0][:, 0:P].rearrange("(k p) n -> p k n", p=P)).then_inc(slot_in[0], 16)
                    sp.wait_ge(F["b_pe"].sem, F["b_pe"].at(NFF - 1, 3))
                    sp.dma_start(ring_raw[R_SLOT][:, 0:KD * RANK].rearrange("p (k n) -> p k n", k=KD),
                                 A["gla_w_in"][0][:, WR:WR + RANK].rearrange("(k p) n -> p k n", p=P)
                                 ).then_inc(slot_in[R_SLOT], 16)
                    sp.dma_start(att["g"]["norm"][:, :], A["gla_norm_g"][0].partition_broadcast(P)).then_inc(const_in, 16)
                    sp.dma_start(att["g"]["wgk"][:, :], A["gla_w_gk2"][0][:, 0:P]).then_inc(SIG["g"]["wgk_in"].sem, 16)
                    sp.dma_start(att["g"]["bgk"][:, :], A["gla_b_gk2"][0].rearrange("(h p) -> p h", p=P)).then_inc(const_in, 16)
                F = FSIG["tail"].layer(layer, NFF)
                sp.wait_ge(F.sem, F.at(NFF - 1, 2))
                lnrows(layer, "ffn", ln_ffn)
                sp.wait_ge(tails_cp, 6 * (layer + 1))
                sp.dma_start(out["conv_p"][layer, 0], tails_out[0:2, :]).then_inc(tails_dma, 16)
                sp.dma_start(out["conv_s"][layer].rearrange("b j f -> (b j) f"), tails_out[2:TAILS, :]).then_inc(tails_dma, 16)

            attention(KIND["h"], 0, True)
            with sp.Fori(1, HEADS_H) as i:
                attention(KIND["h"], i, False)
            out_units(KIND["h"], A["hgrn_w_out"][0])
            before_ffn(KIND["h"], 0, lambda t: A["x_prompt"][0, t * P:(t + 1) * P, :] if t < PT
                       else A["x_sample"].rearrange("b s d -> (b s) d"))
            ffn(0)
            for t in range(NT):
                if t == NT - 2:
                    sp.wait_ge(FSIG["down"].sem, DOWN_ALL)
                    sp.dma_start(ring_raw[1][:, :].rearrange("p (k n) -> p k n", k=KD),
                                 A["gla_w_in"][0][:, D // 2:D // 2 + P].rearrange("(k p) n -> p k n", p=P)).then_inc(slot_in[1], 16)
                sp.wait_ge(ln_done, NT + t + 1)
                sp.dma_start(x2_dram[t * P:(t + 1) * P, :], tm[:, t, :]).then_inc(res_io[t], 16)
            attention(KIND["g"], 0, True)
            with sp.Fori(1, HEADS_G) as i:
                attention(KIND["g"], i, False)
            out_units(KIND["g"], A["gla_w_out"][0])
            before_ffn(KIND["g"], 1, lambda t: x2_dram[t * P:(t + 1) * P, :])
            ffn(1)
            for t in range(NT):
                sp.wait_ge(ln_done, 3 * NT + t + 1)
                dst = out["y_prompt"][0, t * P:(t + 1) * P, :] if t < PT else out["y_sample"].rearrange("b s d -> (b s) d")
                sp.dma_start(dst, tm[:, t, :]).then_inc(y_out, 16)
            sp.wait_ge(y_out, 16 * NT)
            sp.wait_ge(tails_dma, 64)
            for name in ("state_out", "stream_out"):
                sp.wait_ge(SIG["g"][name].sem, SIG["g"][name].at(HEADS_G, 0))

        @block.gpsimd
        def _(pool):
            pool.wait_ge(start_dve, 1)
            pool.memset(att["h"]["a"][:, :, :], 0.0)
            pool.memset(att["h"]["qz"][:, :, :], 0.0).then_inc(start_pool, 1)

            def split(unit, slot, count, width=UNIT, by_act=0, skipped=0):
                if by_act:
                    pool.wait_ge(w_hi, by_act)
                    nc.gpsimd.tensor_tensor(ring_lo[slot][:, 0:width], ring_raw[slot][:, 0:width],
                                            ring_hi[slot][:, 0:width].bitcast(F32), ALU.subtract).then_inc(unit_split, 1)
                    return
                pool.wait_ge(slot_in[slot], count)
                nc.gpsimd.tensor_tensor(ring_hi[slot][:, 0:width], ring_raw[slot][:, 0:width],
                                        ones[:, :].to_broadcast([P, width]), ALU.mult).then_inc(unit_hi, 1)
                pool.wait_ge(unit_hi, unit + (1 - skipped))
                nc.gpsimd.tensor_tensor(ring_lo[slot][:, 0:width], ring_raw[slot][:, 0:width],
                                        ring_hi[slot][:, 0:width].bitcast(F32), ALU.subtract).then_inc(unit_split, 1)

            def add_shift(layer):
                pool.wait_ge(lnrow_in, 32 * (2 * layer + 2))
                for t in range(NT):
                    pool.wait_ge(ln_scaled, layer * NT + t + 1)
                    nc.gpsimd.tensor_tensor(tm[:, t, :], tm[:, t, :], ln_ffn[1][:, :], ALU.add).then_inc(ln_done, 1)

            def head_units(K, i, s0=0):
                for s in range(s0, K["units"]):
                    split(i * K["units"] + (K["unit0"] + s), s, slot_count(K["n"], i, s), skipped=(0 if K["n"] == "h" else 4))

            def out_units(layer, base, unit0):
                for u, slot in enumerate(W_SLOTS):
                    split(unit0 + u, slot, 16 * (base[slot] + 1), by_act=(4 * layer + u - 3 if u >= 4 else 0), skipped=4 * layer)

            def ffn_units(base, unit0, skipped):
                def up(j, unit):
                    for s in range(4):
                        split(unit + s, s, (j + 1) * 16 + 16 * base[s], skipped=skipped)

                def down(j, unit):
                    for u, slot in enumerate(DOWN_SLOTS):
                        split(unit + u, slot, (j + 1) * 16 + 16 * base[slot], skipped=skipped)

                up(0, unit0)
                with pool.Fori(1, GROUPS) as j:
                    up(j, j * 6 + (unit0 - 2))
                    down(j - 1, j * 6 + (unit0 + 2))
                for u, slot in enumerate(DOWN_SLOTS_LAST):
                    split(unit0 + (6 * GROUPS - 2 + u), slot, 16 * (base[slot] + GROUPS + 1), skipped=skipped)

            with pool.Fori(0, HEADS_H) as i:
                head_units(KIND["h"], i)
            out_units(0, slot_base["wh"], U_WH)
            ffn_units(slot_base["f0"], U_F0, 4)
            split(U_R, R_SLOT, 16 * (slot_base["r"][R_SLOT] + 1), KD * RANK, skipped=4)
            split(U_G, 0, slot_count("g", 0, 0), skipped=4)
            add_shift(0)
            split(U_G + 1, 1, slot_count("g", 0, 1), skipped=4)
            pool.wait_ge(FSIG["down"].sem, DOWN_ALL)
            pool.wait_ge(ln_done, 2 * NT)
            pool.memset(att["g"]["a"][:, :, :], 0.0)
            pool.memset(att["g"]["qz"][:, :, :], 0.0).then_inc(start_pool, 1)
            head_units(KIND["g"], 0, 2)
            with pool.Fori(1, HEADS_G) as i:
                head_units(KIND["g"], i)
            out_units(1, slot_base["wg"], U_WG)
            ffn_units(slot_base["f1"], U_F1, 8)
            add_shift(1)

        @block.tensor
        def _(pe):
            def mm3(dst, w_hi, w_lo, x_hi, x_lo, start, stop):
                nc.tensor.matmul(dst, w_hi, x_hi, start=start, stop=False)
                nc.tensor.matmul(dst, w_hi, x_lo, start=False, stop=False)
                return nc.tensor.matmul(dst, w_lo, x_hi, start=False, stop=stop)

            def project_feature_major(slot, banks, done, before=None, chunks=range(NC)):
                for c in chunks:
                    if before:
                        before(c)
                    for k in range(KD):
                        last = mm3(bank[banks[c]][:, 0:CH], ring_hi[slot][:, k * P:(k + 1) * P], ring_lo[slot][:, k * P:(k + 1) * P],
                                   xt_hi[:, k, c * CH:(c + 1) * CH], xt_lo[:, k, c * CH:(c + 1) * CH],
                                   k == 0, k == KD - 1)
                    last.then_inc(done, 1)

            def transpose_tile(t, job, b0=4):
                for hf in range(2):
                    if job + hf >= 2:
                        pe.wait_ge(tj_lo, job + hf - 1)
                    for k in range(4):
                        kk = 4 * hf + k
                        last = nc.tensor.transpose(bank[b0 + hf][:, k * P:(k + 1) * P], tm[:, t, kk * P:(kk + 1) * P], ident[:, :])
                    last.then_inc(tj_done, 1)

            def attention(K, i, first, last_):
                n, dv = K["n"], K["dv"]
                S, tile = SIG[n], att[n]
                U = i * K["units"] + K["unit0"]
                npj = S["kvp_pe"].per

                def wait(name, it, k):
                    pe.wait_ge(S[name].sem, S[name].at(it, k))

                if not last_ and not first:
                    pe.wait_ge(unit_split, U + 1)
                    wait("pred", i - 1, S["pred"].per)
                    project_feature_major(0, (0, 1, 2), S[K["first"] + "_proj"].sem)
                elif first and n == "h":
                    for c in range(NC):
                        for t in range(c * TPC, (c + 1) * TPC):
                            pe.wait_ge(x_in[t], 16)
                            transpose_tile(t, 2 * t, 6)
                        pe.wait_ge(tj_lo, 2 * TPC * (c + 1))
                        for slot, banks, x in ((0, (0, 1, 2), "first"), (1, SECOND_BANKS, "second")):
                            if c == 0:
                                pe.wait_ge(unit_split, slot + 1)
                            project_feature_major(slot, banks, S[K[x] + "_proj"].sem, chunks=(c,))
                if not first:
                    p = i - 1
                    wait("kh", p, 1)
                    wait("vg", p, NT)
                    if last_:
                        wait("pred", p, S["pred"].per)
                    for jb, (b, tiles) in enumerate(((6, range(0, 4)), (3, range(4, 8)), (4, range(8, 9)))):
                        for x, t in enumerate(tiles):
                            last = nc.tensor.transpose(bank[b][:, x * P:(x + 1) * P], tile["c0"][:, t * P:(t + 1) * P], ident[:, :])
                        last.then_inc(S["kt_pe"].sem, 1)
                    for t in range(NT):
                        last = nc.tensor.matmul(bank[7][:, t:t + 1], tile["c1"][:, t * P:(t + 1) * P], ones[:, :],
                                                start=True, stop=True)
                    last.then_inc(S["dots_pe"].sem, 1)
                    wait("kt", p, 3)
                    per_job = 512 // dv
                    for jb, b in zip(range(npj), (5, 6, 3, 4)):
                        for x in range(per_job):
                            c = jb * per_job + x
                            last = nc.tensor.matmul(bank[b][:, x * dv:(x + 1) * dv], tile["kt"][:, c, :], tile["v"][:, c, :],
                                                    start=True, stop=True)
                        last.then_inc(S["kvp_pe"].sem, 1)
                    wait("dots", p, 1)
                    wait("qz", p, 1)
                    pe.wait_ge(S["s0_in"].sem, S["s0_in"].at(p, 16))
                    nc.tensor.matmul(bank[7][:, 0:dv], tile["a"][:, PT, :], tile["v"][:, PT, :], start=True, stop=False)
                    for s in range(STREAMS):
                        last = nc.tensor.matmul(bank[7][:, 0:dv], tile["qz"][:, s, :], tile["s0"][:, s, :],
                                                start=False, stop=(s == STREAMS - 1))
                    last.then_inc(S["odec_pe"].sem, 1)
                    wait("vz", p, 1)
                    for jb, b in zip(range(npj), (3, 4) if n == "h" else (5, 6, 3, 4)):
                        if n == "g":
                            wait("chain", p, (jb + 1) * per_job)
                        last = nc.tensor.matmul(bank[b][:, :], tile["kt"][:, PT, :],
                                                tile["vz"][:, :, :].rearrange("p s v -> p (s v)")[:, jb * 512:(jb + 1) * 512],
                                                start=True, stop=True)
                        last.then_inc(S["kvd_pe"].sem, 1)
                if n == "g" and not last_:
                    pe.wait_ge(S["wgk_in"].sem, S["wgk_in"].at(i, 16))
                    pe.wait_ge(S["rt"].sem, 3)
                    for c in range(NC):
                        wait("q_ready", i, c + 1)
                        nc.tensor.matmul(bank[c][:, 0:CH].rearrange("p (t n) -> p t n", n=P), tile["wgk"][:, :],
                                         rt[:, c * TPC:(c + 1) * TPC, :], start=True, stop=True).then_inc(S["z_proj"].sem, 1)
                if not last_ and not (first and n == "h"):
                    pe.wait_ge(unit_split, U + 2)

                    def bank_ready(c):
                        if n == "h" and c == 0:
                            wait("chain", i - 1, 512 // dv)
                        else:
                            wait("s0new", i - 1, {"h": (0, 4, 8), "g": (2, 6, 8)}[n][c])
                    project_feature_major(1, SECOND_BANKS, S[K["second"] + "_proj"].sem, before=(None if first else bank_ready))
                if not first:
                    p = i - 1
                    wait("chain", p, PT)
                    wait("qh", p, 1)
                    wait("o_add", p, 1)
                    if n == "g":
                        wait("s0new", p, STREAMS)
                    for jb in range(npj):
                        if jb >= 2:
                            wait("o_add", p, 1 + (jb - 1) * per_job)
                        for x in range(per_job):
                            c = jb * per_job + x
                            dst = bank[6 + jb % 2][:, x * dv:(x + 1) * dv]
                            last = nc.tensor.matmul(dst, tile["a"][:, c, :], tile["v"][:, c, :], start=True, stop=(c == 0))
                            if c > 0:
                                last = nc.tensor.matmul(dst, tile["qh"][:, c * P:(c + 1) * P], tile["chain"][:, c - 1, :],
                                                        start=False, stop=True)
                        last.then_inc(S["o_pe"].sem, 1)
                if not last_:
                    kk = UNIT // (2 * dv)
                    order = MERGED[1:3] + MERGED[:1] + MERGED[3:] if first else MERGED
                    for what, x in order:
                        if what == "vg":
                            if x == 0:
                                pe.wait_ge(unit_split, U + K["units"])
                            if x < 2 and not first:
                                wait("o_add", i - 1, NT if x else NT - 512 // dv)
                            if x >= 2:
                                wait("vg", i, x - 1)
                            dst = vg_dst(dv, x)
                            for k in range(KD):
                                s, c = 2 + k // kk, (k % kk) * 2 * dv
                                xh, xl = xt_hi[:, k, x * P:(x + 1) * P], xt_lo[:, k, x * P:(x + 1) * P]
                                last = mm3(dst, xh, xl, ring_hi[s][:, c:c + 2 * dv], ring_lo[s][:, c:c + 2 * dv],
                                           k == 0, k == KD - 1)
                            last.then_inc(S["vg_pe"].sem, 1)
                        else:
                            c = tile["c0"] if x % 2 == 0 else tile["c1"]
                            if x == 0:
                                wait("k_sig" if n == "h" else "k_ready", i, 3 if n == "h" else 1)
                                wait("q_ready" if n == "h" else "z_min", i, 3)
                            wait("lvl", i, x + 1)
                            if x >= 2:
                                wait("pred", i, preds_after(x - 2))
                            for t in range(PT + (1 if x >= DEC_FROM else 0)):
                                ct = c[:, t * P:(t + 1) * P]
                                last = nc.tensor.matmul(scores(x, t), ct, ct, start=True, stop=True)
                            last.then_inc(S["lvl_pe"].sem, 1)

            def out_projection(layer, unit0):
                S, heads = (SIG["h"], HEADS_H) if layer == 0 else (SIG["g"], HEADS_G)
                pe.wait_ge(S["final"].sem, S["final"].at(heads, 0))
                for t in range(2):
                    transpose_tile(t, w_job(layer, "o", t))
                for t in range(NT):
                    for half in range(2):
                        n = (layer * NT + t) * 2 + half
                        if t == 0:
                            pe.wait_ge(unit_split, unit0 + 4 * (half + 1))
                        if half == 0:
                            pe.wait_ge(tj_lo, w_job(layer, "o", t) + 2)
                        if n >= 2:
                            pe.wait_ge(w_added, n - 1)
                        for k in range(KD):
                            s, c = W_SLOTS[4 * half + k // 2], (k % 2) * 512
                            last = mm3(bank[6 + half][:, :], xt_hi[:, k, t * P:(t + 1) * P], xt_lo[:, k, t * P:(t + 1) * P],
                                       ring_hi[s][:, c:c + 512], ring_lo[s][:, c:c + 512], k == 0, k == KD - 1)
                        last.then_inc(w_done, 1)
                        for x in O_AHEAD[t] if half == 0 else ():
                            transpose_tile(x, w_job(layer, "o", x))
                        if half == 1 and t >= 1:
                            pe.wait_ge(ln_done, 2 * layer * NT + t)
                            transpose_tile(t - 1, w_job(layer, "n", t - 1))

            def ffn(layer, unit0):
                F = {k: v.layer(layer, NFF) for k, v in FSIG.items()}
                DN, AD = ffn_sums(layer)

                pe.wait_ge(rows_sem, 48 * (layer + 1))
                pe.wait_ge(w_added, (2 * layer + 2) * NT)
                for f in range(NFF):
                    last = nc.tensor.transpose(bank[3][:, f * ROWS:(f + 1) * ROWS], rows_in[:, f * P:(f + 1) * P],
                                               ident[0:ROWS, 0:ROWS])
                last.then_inc(DN.sem, 1)

                def up(j, unit, first=False):
                    for u in range(2):
                        f = j * 2 + u
                        pe.wait_ge(unit_split, unit + (2 * u + 1))
                        pe.wait_ge(F["a_out"].sem, F["a_out"].at(f, 0))

                        def ready(c):
                            if first and u == 0:
                                if c == NC - 1:
                                    pe.wait_ge(ln_done, (2 * layer + 1) * NT)
                                    transpose_tile(NT - 1, w_job(layer, "n", NT - 1))
                                pe.wait_ge(tj_lo, w_job(layer, "n", TPC * (c + 1) - 1) + 2)
                        project_feature_major(2 * u, (0, 1, 2), F["a_pe"].sem, before=ready)
                        pe.wait_ge(unit_split, unit + (2 * u + 2))
                        if first and u == 0:
                            pe.wait_ge(params_rd, layer + 1)
                        pe.wait_ge(F["mult"].sem, F["mult"].at(f, 0))
                        project_feature_major(2 * u + 1, (3, 4, 5), F["b_pe"].sem)

                def down_tile(t, n, parts, start, stop):
                    for x, (g, u, slot) in enumerate(parts):
                        last = mm3(bank[6 + n][:, :], h_hi[g][u][:, t * P:(t + 1) * P], h_lo[g][u][:, t * P:(t + 1) * P],
                                   ring_hi[slot][:, n * 512:(n + 1) * 512], ring_lo[slot][:, n * 512:(n + 1) * 512],
                                   start and x == 0, stop and x == len(parts) - 1)
                    return last

                def down(j, g, unit):
                    pe.wait_ge(unit_split, unit + 2)
                    pe.wait_ge(F["h_lo"].sem, F["h_lo"].at(j * 2 + 1, 1))
                    parts = [(g, u, DOWN_SLOTS[u]) for u in range(2)]
                    for t in range(NT):
                        for n in range(2):
                            pe.wait_ge(AD.sem, AD.at(j, max(0, 2 * t + n - 1)))
                            down_tile(t, n, parts, True, True).then_inc(DN.sem, 1)

                def down_last(unit):
                    j = GROUPS - 2
                    parts = [(j % 2, u, DOWN_SLOTS[u]) for u in range(2)]
                    parts_last = [((j + 1) % 2, u, DOWN_SLOTS_LAST[u]) for u in range(2)]
                    pe.wait_ge(unit_split, unit + 2)
                    pe.wait_ge(F["h_lo"].sem, F["h_lo"].at(j * 2 + 1, 1))
                    for t in range(NT):
                        for n in range(2):
                            pe.wait_ge(AD.sem, AD.at(j, max(0, 2 * t + n - 1)))
                            down_tile(t, n, parts, True, False)
                            if t == 0 and n == 0:
                                pe.wait_ge(unit_split, unit0 + 6 * GROUPS)
                                pe.wait_ge(F["h_lo"].sem, F["h_lo"].at(NFF - 1, 1))
                            down_tile(t, n, parts_last, False, True).then_inc(DN.sem, 1)
                            if layer == 0 and n == 0 and t >= 2:
                                next_operand(t - 2)
                        if layer == 0 and t >= TPC + 2 and (t - TPC - 2) % TPC == 0:
                            gla_first((t - TPC - 2) // TPC)

                def next_operand(t):
                    pe.wait_ge(ln_done, NT + t + 1)
                    transpose_tile(t, JOB_G + 2 * t)

                def gla_first(c):
                    S = SIG["g"]
                    pe.wait_ge(tj_lo, JOB_G + 2 * TPC * (c + 1))
                    if c == 0:
                        pe.wait_ge(unit_split, U_G + 1)
                        pe.wait_ge(tails_cp, 6)
                    else:
                        pe.wait_ge(S["rt"].sem, c)
                    for b, slot, width, done in ((3, R_SLOT, RANK, "r_pe"), (c, 0, P, "q_proj")):
                        for k in range(KD):
                            last = mm3(bank[b][0:width, 0:CH],
                                       ring_hi[slot][:, k * width:(k + 1) * width], ring_lo[slot][:, k * width:(k + 1) * width],
                                       xt_hi[:, k, c * CH:(c + 1) * CH], xt_lo[:, k, c * CH:(c + 1) * CH], k == 0, k == KD - 1)
                        last.then_inc(S[done].sem, 1)

                up(0, unit0, True)
                with pe.Fori(0, GROUPS // 2 - 1) as pair:
                    j = pair * 2 + 1
                    up(j, j * 6 + (unit0 - 2))
                    down(j - 1, 0, j * 6 + (unit0 + 2))
                    up(j + 1, j * 6 + (unit0 + 4))
                    down(j, 1, j * 6 + (unit0 + 8))
                j = GROUPS - 2
                up(j, j * 6 + (unit0 - 2))
                down(j - 1, 0, j * 6 + (unit0 + 2))
                up(j + 1, j * 6 + (unit0 + 4))
                pe.wait_ge(F["tail"].sem, F["tail"].at(NFF - 1, 2))
                pe.wait_ge(F["a_out"].sem, F["a_out"].at(NFF - 1, 3))
                for b in range(6):
                    if b >= 3:
                        pe.wait_ge(tails_cp, 6 * layer + b - 2)
                    for x in range(4 if b < 5 else 2):
                        f = 4 * b + x
                        last = nc.tensor.transpose(bank[b % 3][0:TAILS, x * P:(x + 1) * P], tails[:, f, :], ident[:, :])
                    last.then_inc(tails_pe, 1)

                pe.wait_ge(F["mult"].sem, F["mult"].at(NFF - 1, 3))
                down_last(j * 6 + (unit0 + 8))
                if layer == 0:
                    for t in (NT - 2, NT - 1):
                        next_operand(t)
                    gla_first(NC - 1)

            pe.wait_ge(ident_in, 16)
            pe.wait_ge(start_dve, 1)
            attention(KIND["h"], 0, True, False)
            with pe.Fori(1, HEADS_H) as i:
                attention(KIND["h"], i, False, False)
            attention(KIND["h"], HEADS_H, False, True)
            out_projection(0, U_WH)
            ffn(0, U_F0)
            attention(KIND["g"], 0, True, False)
            with pe.Fori(1, HEADS_G) as i:
                attention(KIND["g"], i, False, False)
            attention(KIND["g"], HEADS_G, False, True)
            out_projection(1, U_WG)
            ffn(1, U_F1)

        @block.scalar
        def _(act):
            def activate(*a, **k):
                return nc.scalar.activation(*a, **k)

            def take_transposed(t, job, b0=4):
                for hf in range(2):
                    act.wait_ge(tj_done, job + hf + 1)
                    activate(xt_hi[:, 4 * hf:4 * hf + 4, t * P:(t + 1) * P],
                             bank[b0 + hf][:, :].rearrange("p (k n) -> p k n", k=4), ACT.Copy).then_inc(tj_hi, 1)

            def ln_std_of(t, n):
                act.wait_ge(ln_moments, n + 1)
                activate(std[:, t:t + 1], moments[:, t, 1:2], ACT.Sqrt, bias=eps_ln[:, :]).then_inc(ln_sqrt, 1)

            def attention(K, i, first, last_):
                n, dv = K["n"], K["dv"]
                S, tile = SIG[n], att[n]

                def wait(name, it, k):
                    act.wait_ge(S[name].sem, S[name].at(it, k))

                def cols(c):
                    return slice(c * CH, (c + 1) * CH)

                def token_keys():
                    p = i - 1
                    for jb, (b, t0, t1) in enumerate(((6, 0, 4), (3, 4, 8), (4, 8, 9))):
                        wait("kt_pe", p, jb + 1)
                        activate(tile["kt"][:, t0:t1, :], bank[b][:, 0:(t1 - t0) * P].rearrange("p (t n) -> p t n", n=P),
                                 ACT.Copy).then_inc(S["kt"].sem, 1)

                def level(x):
                    m, c = LEVELS[x], tile["c0"] if x % 2 == 0 else tile["c1"]
                    v = blocks(c, m, level_tokens(x))
                    wait("sub", i, x + 1)
                    activate(v[:, :, 0:m], v[:, :, 0:m], ACT.Exp, scale=-K["scale"])
                    activate(v[:, :, m:2 * m], v[:, :, m:2 * m], ACT.Exp, scale=K["scale"]).then_inc(S["exp"].sem, 1)

                def squares():
                    p = i - 1
                    for x, t in enumerate([PT] + list(range(PT))):
                        wait("o_add", p, x + 1)
                        if x > 0:
                            wait("squares", p, x)
                        activate(tile["junk"][:, :], tile["v"][:, t, :], ACT.Square, accum_out=tile["ss"][:, t:t + 1]
                                 ).then_inc(S["squares"].sem, 1)

                def rms():
                    p = i - 1
                    wait("squares", p, NT)
                    activate(tile["rms"][:, :], tile["ss"][:, :], ACT.Sqrt, scale=1.0 / dv, bias=eps_rms[:, :]).then_inc(S["rms"].sem, 1)

                def take_vg(t):
                    wait("vg_pe", i, t + 1)
                    if t == 0 and not first:
                        wait("gated_o", i - 1, 1)
                        wait("squares", i - 1, NT)
                    if first and n == "g":
                        act.wait_ge(res_io[t], 32)
                    src = vg_dst(dv, t)
                    activate(tile["v"][:, t, :], src[:, 0:dv], ACT.Copy)
                    activate(tm[:, t, bass.ds(i * dv, dv)], src[:, dv:2 * dv], ACT.Copy).then_inc(S["vg"].sem, 1)

                if last_:
                    token_keys()
                if not first:
                    wait("vg", i - 1, NT)
                    g = tm[:, :, bass.ds((i - 1) * dv, dv)]
                    if n == "h":
                        activate(tile["gt"][:, :, :], g, ACT.Sigmoid).then_inc(S["g_act"].sem, 1)
                    else:
                        activate(g, g, ACT.Silu).then_inc(S["g_act"].sem, 1)
                if n == "h":
                    if not first and not last_:
                        token_keys()
                    if not last_:
                        if not first:
                            wait("kvd_pe", i - 1, S["kvd_pe"].per)
                        for c in range(NC):
                            wait("k_proj", i, c + 1)
                            activate(tile["c1"][:, cols(c)], bank[c][:, 0:CH], ACT.Sigmoid).then_inc(S["k_sig"].sem, 1)
                        wait("forget", i, 1)
                        activate(tile["c0"][:, :], tile["c1"][:, :], ACT.Ln).then_inc(S["log_f"].sem, 1)
                        level(0)
                        for c in range(NC):
                            wait("q_proj", i, c + 1)
                            activate(tile["q"][:, cols(c)], bank[SECOND_BANKS[c]][:, 0:CH], ACT.Sigmoid).then_inc(S["q_sig"].sem, 1)
                else:
                    if not last_:
                        if not first:
                            wait("qh", i - 1, 1)
                        for c in range(NC):
                            wait("q_proj", i, c + 1)
                            activate(tile["q"][:, cols(c)], bank[c][:, 0:CH], ACT.Copy, scale=float(P) ** -0.5
                                     ).then_inc(S["q_ready"].sem, 1)
                        activate(tile["bcol"][:, :], tile["bgk"][:, bass.ds(i, 1)], ACT.Copy).then_inc(S["bcol"].sem, 1)
                    if not first and not last_:
                        token_keys()
                    if not last_:
                        if not first:
                            wait("kvd_pe", i - 1, S["kvd_pe"].per)
                        wait("bcol", i, 1)
                        for c in range(NC):
                            wait("z_proj", i, c + 1)
                            activate(tile["c0"][:, cols(c)], bank[c][:, 0:CH], ACT.Abs, bias=tile["bcol"][:, :]
                                     ).then_inc(S["z_abs"].sem, 1)
                        wait("z_abs", i, 3)
                        activate(tile["c0"][:, :], tile["c0"][:, :], ACT.Exp, scale=-1.0).then_inc(S["z_exp"].sem, 1)
                        wait("z_exp", i, 1)
                        activate(tile["c0"][:, :], tile["c0"][:, :], ACT.Ln, bias=ones[:, :]).then_inc(S["z_log"].sem, 1)
                        level(0)
                        for c in range(NC):
                            wait("k_proj", i, c + 1)
                            last = activate(tile["k"][:, cols(c)], bank[SECOND_BANKS[c]][:, 0:CH], ACT.Copy)
                        last.then_inc(S["k_ready"].sem, 1)
                if not first:
                    squares()
                if last_:
                    rms()
                    return
                for t in range(NL - 1):
                    level(t + 1)
                    take_vg(t)
                if not first:
                    wait("o_add", i - 1, NT)
                    act.wait_ge(S["state_out"].sem, S["state_out"].at(i - 1, 16))
                activate(tile["e"][:, :], tile["b"][:, :], ACT.Exp, scale=K["scale"]).then_inc(S["e"].sem, 1)
                take_vg(NL - 1)
                wait("kh_sub", i, 2)
                activate(tile["c0"][:, :], tile["c0"][:, :], ACT.Exp, scale=-K["scale"]).then_inc(S["kh_exp"].sem, 1)
                for t in range(NL, NT):
                    take_vg(t)
                if not first:
                    rms()

            def out_projection(layer):
                for u in range(4, 8):
                    slot = W_SLOTS[u]
                    if u == 7:
                        for t in range(2):
                            take_transposed(t, w_job(layer, "o", t))
                    act.wait_ge(slot_in[slot], 16 * (slot_base["wh" if layer == 0 else "wg"][slot] + 1))
                    activate(ring_hi[slot][:, :], ring_raw[slot][:, :], ACT.Copy).then_inc(w_hi, 1)
                for t in range(NT):
                    for x in O_AHEAD[t]:
                        take_transposed(x, w_job(layer, "o", x))
                    if t >= 1:
                        take_transposed(t - 1, w_job(layer, "n", t - 1))
                    ln_std_of(t, 2 * layer * NT + t)
                take_transposed(NT - 1, w_job(layer, "n", NT - 1))

            def ffn(layer):
                F = {k: v.layer(layer, NFF) for k, v in FSIG.items()}
                DN, _ = ffn_sums(layer)

                def wait(name, f, k):
                    act.wait_ge(F[name].sem, F[name].at(f, k))

                def tile(j, u, g, first=False):
                    f = j * 2 + u
                    for c in range(NC):
                        wait("a_pe", f, c + 1)
                        if c == 0 and not first:
                            wait("tail", f - 2, 2)
                        n = min(PROMPT, (c + 1) * CH) - c * CH
                        last = activate(ax[u][:, 2 + c * CH:2 + c * CH + n], bank[c][:, 0:n], ACT.Copy)
                        if n < CH:
                            dst = ax[u][:, 2 + PROMPT:].rearrange("p (s w) -> p s w", s=STREAMS)[:, :, 2:]
                            last = activate(dst, bank[c][:, n:CH].rearrange("p (s w) -> p s w", s=STREAMS), ACT.Copy)
                        last.then_inc(F["a_out"].sem, 1)
                    wait("conv", f, 3)
                    activate(cv[u][:, :], cv[u][:, :], ACT.Gelu_apprx_tanh).then_inc(F["gelu"].sem, 1)
                    wait("mult", f, 3)
                    if not first:
                        act.wait_ge(DN.sem, DN.at(j - 1, 0))
                    activate(h_hi[g][u][:, :], cv[u][:, :], ACT.Copy).then_inc(F["h_hi"].sem, 1)

                tile(0, 0, 0, True)
                tile(0, 1, 0, True)
                with act.Fori(0, GROUPS // 2) as pair:
                    j = pair * 2 + 1
                    for u in range(2):
                        tile(j, u, 1)
                    for u in range(2):
                        tile(j + 1, u, 0)
                for b in range(6):
                    act.wait_ge(tails_pe, 6 * layer + b + 1)
                    w = 512 if b < 5 else 256
                    activate(tails_out[:, b * 512:b * 512 + w], bank[b % 3][0:TAILS, 0:w], ACT.Copy).then_inc(tails_cp, 1)
                def take_r(c):
                    for x in range(c * TPC, (c + 1) * TPC):
                        act.wait_ge(res_io[x], 32)
                    act.wait_ge(SIG["g"]["r_pe"].sem, c + 1)
                    activate(rt[:, c * TPC:(c + 1) * TPC, :], bank[3][0:RANK, 0:CH].rearrange("p (t n) -> p t n", n=P),
                             ACT.Copy).then_inc(SIG["g"]["rt"].sem, 1)

                for t in range(NT):
                    if layer == 0 and t >= 2:
                        take_transposed(t - 2, JOB_G + 2 * (t - 2))
                    act.wait_ge(ln_neg, layer * NT + t + 1)
                    activate(tm[:, t, :], tm[:, t, :], ACT.Identity, bias=neg_mean[:, t:t + 1]).then_inc(ln_centered, 1)
                    ln_std_of(t, (2 * layer + 1) * NT + t)
                    if layer == 0 and t >= TPC + 2 and (t - TPC - 2) % TPC == 0:
                        take_r((t - TPC - 2) // TPC)
                if layer == 0:
                    for t in (NT - 2, NT - 1):
                        take_transposed(t, JOB_G + 2 * t)
                    take_r(NC - 1)

            act.wait_ge(start_dve, 1)
            for t in range(NT):
                take_transposed(t, 2 * t, 6)
            act.wait_ge(prep, 2)
            activate(att["h"]["lbx"][:, :, :], att["h"]["lbx"][:, :, :], ACT.Exp).then_inc(prep, 1)
            attention(KIND["h"], 0, True, False)
            with act.Fori(1, HEADS_H) as i:
                attention(KIND["h"], i, False, False)
            attention(KIND["h"], HEADS_H, False, True)
            out_projection(0)
            ffn(0)
            act.wait_ge(const_in, 16 * 9)
            attention(KIND["g"], 0, True, False)
            with act.Fori(1, HEADS_G) as i:
                attention(KIND["g"], i, False, False)
            attention(KIND["g"], HEADS_G, False, True)
            out_projection(1)
            ffn(1)

        @block.vector
        def _(dve):
            V = nc.vector

            def take_transposed(t, job, b0=4):
                for hf in range(2):
                    dve.wait_ge(tj_hi, job + hf + 1)
                    V.tensor_tensor(xt_lo[:, 4 * hf:4 * hf + 4, t * P:(t + 1) * P],
                                    bank[b0 + hf][:, :].rearrange("p (k n) -> p k n", k=4),
                                    xt_hi[:, 4 * hf:4 * hf + 4, t * P:(t + 1) * P].bitcast(F32), ALU.subtract).then_inc(tj_lo, 1)

            def ln_stats(t, n):
                for hf in range(2):
                    last = V.bn_stats(stats[:, t % 2, hf, :], tm[:, t, hf * 512:(hf + 1) * 512])
                last.then_inc(ln_step, 1)
                dve.wait_ge(ln_step, n + 1)
                V.bn_aggr(moments[:, t, :], stats[:, t % 2, :, :]).then_inc(ln_moments, 1)

            def ln_apply(t, layer):
                n = 2 * layer * NT + t
                dve.wait_ge(ln_sqrt, n + 1)
                V.reciprocal(inv_std[:, t:t + 1], std[:, t:t + 1]).then_inc(ln_std, 1)
                V.scalar_tensor_tensor(tm[:, t, :], tm[:, t, :], moments[:, t, 0:1], ln_att[0][:, :], ALU.subtract, ALU.mult
                                       ).then_inc(ln_a, 1)
                dve.wait_ge(ln_std, n + 1)
                dve.wait_ge(ln_a, layer * NT + t + 1)
                V.scalar_tensor_tensor(tm[:, t, :], tm[:, t, :], inv_std[:, t:t + 1], ln_att[1][:, :], ALU.mult, ALU.add
                                       ).then_inc(ln_done, 1)

            def attention(K, i, first, last_):
                n, dv = K["n"], K["dv"]
                S, tile = SIG[n], att[n]

                def wait(name, it, k):
                    dve.wait_ge(S[name].sem, S[name].at(it, k))

                def cols(c):
                    return slice(c * CH, (c + 1) * CH)

                if not first:
                    p = i - 1
                    if not last_:
                        gate(K, p)
                    wait("dots_pe", p, 1)
                    V.tensor_copy(tile["dot"][:, :], bank[7][:, 0:NT]).then_inc(S["dots"].sem, 1)
                    chain_tail(K, p)
                    if last_ and n == "g":
                        gate(K, p)
                if not last_:
                    if n == "h":
                        wait("k_sig", i, 3)
                        V.tensor_scalar(tile["c1"][:, :], tile["c1"][:, :], tile["span"][:, bass.ds(i, 1), 0],
                                        tile["floor"][:, bass.ds(i, 1), 0], ALU.mult, ALU.add).then_inc(S["forget"].sem, 1)
                        wait("forget", i, 1)
                        V.tensor_scalar(tile["k"][:, :], tile["c1"][:, :], -1.0, 1.0, ALU.mult, ALU.add).then_inc(S["forget"].sem, 1)
                        wait("log_f", i, 1)
                        src = tile["c0"]
                    else:
                        for c in range(NC):
                            wait("z_abs", i, c + 1)
                            V.tensor_scalar(tile["c1"][:, cols(c)], bank[c][:, 0:CH], tile["bcol"][:, :], 0.0,
                                            ALU.add, ALU.min).then_inc(S["z_min"].sem, 1)
                        wait("z_min", i, 3)
                        wait("z_log", i, 1)
                        V.tensor_tensor(tile["c1"][:, :], tile["c1"][:, :], tile["c0"][:, :], ALU.subtract
                                        ).then_inc(S["scan_in"].sem, 1)
                        wait("scan_in", i, 1)
                        src = tile["c1"]
                    V.tensor_tensor_scan(tile["b"][:, :], keep[:, :], src[:, :], 0.0, ALU.mult, ALU.add).then_inc(S["scanned"].sem, 1)
                    wait("scanned", i, 1)

                    def sub(x):
                        m, c = LEVELS[x], tile["c0"] if x % 2 == 0 else tile["c1"]
                        if x >= 2:
                            wait("lvl_pe", i, x - 1)
                            if x >= 3:
                                wait("pred", i, preds_after(x - 3))
                        b = blocks(tile["b"], m, level_tokens(x))
                        V.tensor_tensor(blocks(c, m, level_tokens(x)), b, b[:, :, m - 1:m].to_broadcast([P, b.shape[1], 2 * m]),
                                        ALU.subtract).then_inc(S["sub"].sem, 1)

                    def decay(x):
                        m, c = LEVELS[x], tile["c0"] if x % 2 == 0 else tile["c1"]
                        v = blocks(c, m, level_tokens(x))
                        if x == 0:
                            if n == "g":
                                wait("k_ready", i, 1)
                            else:
                                wait("q_ready", i, 3)
                        wait("exp", i, x + 1)
                        V.tensor_tensor(v[:, :, 0:m], v[:, :, 0:m], blocks(tile["k"], m, level_tokens(x))[:, :, 0:m], ALU.mult)
                        V.tensor_tensor(v[:, :, m:2 * m], v[:, :, m:2 * m], blocks(tile["q"], m, level_tokens(x))[:, :, m:2 * m],
                                        ALU.mult).then_inc(S["lvl"].sem, 1)

                    def place_scores(x):
                        m = LEVELS[x]
                        mask = level_mask[:, x * 64:(x + 1) * 64].rearrange("p (g w) -> p g w", w=m)
                        parts = [(0, 4, bank[2 * (x % 2)]), (4, 8, bank[2 * (x % 2) + 1])]
                        if x >= DEC_FROM:
                            parts.append((PT, NT, bank[4 + x % 2]))
                        for t0, t1, ps in parts:
                            nt = t1 - t0
                            dst = tile["a"][:, t0:t1, :].rearrange("p t (g w) -> p t g w", w=2 * m)[:, :, :, m:2 * m]
                            src = ps[:, 0:nt * P].rearrange("p (t g w) -> p t g w", t=nt, w=2 * m)[:, :, :, m:2 * m]
                            msk = mask.unsqueeze(1).to_broadcast([P, nt, 64 // m, m])
                            V.copy_predicated(dst, msk, src).then_inc(S["pred"].sem, 1)

                    sub(0)
                    if n == "h":
                        for c in range(NC):
                            wait("q_sig", i, c + 1)
                            V.tensor_tensor(tile["q"][:, cols(c)], bank[SECOND_BANKS[c]][:, 0:CH], tile["q"][:, cols(c)], ALU.mult
                                            ).then_inc(S["q_ready"].sem, 1)
                    decay(0)
                if not first:
                    add_diagonal(K, i - 1)
                if last_ and n == "h":
                    gate(K, i - 1)
                if not last_:
                    sub(1)
                if not first:
                    apply_gate(K, i - 1)
                if last_:
                    apply_rms(K, i - 1)
                    return
                decay(1)
                for x in range(2, NL):
                    sub(x)
                    place_scores(x - 2)
                    decay(x)
                wait("lvl_pe", i, NL - 1)
                wait("pred", i, preds_after(NL - 3))
                V.tensor_tensor(tile["c1"][:, :], tile["q"][:, :], tile["k"][:, :], ALU.mult).then_inc(S["prod"].sem, 1)
                place_scores(NL - 2)
                wait("lvl_pe", i, NL)
                wait("pred", i, preds_after(NL - 2))
                bp = tile["b"][:, 0:PROMPT].rearrange("p (t n) -> p t n", n=P)
                bs = tile["b"][:, PROMPT:T].rearrange("p (s n) -> p s n", n=STREAM_T)
                V.tensor_tensor(tile["c0"][:, PROMPT:T].rearrange("p (s n) -> p s n", n=STREAM_T), bs,
                                bs[:, :, STREAM_T - 1:STREAM_T].to_broadcast([P, STREAMS, STREAM_T]), ALU.subtract
                                ).then_inc(S["kh_sub"].sem, 1)
                place_scores(NL - 1)
                V.tensor_tensor(tile["c0"][:, 0:PROMPT].rearrange("p (t n) -> p t n", n=P), bp,
                                bp[:, :, P - 1:P].to_broadcast([P, PT, P]), ALU.subtract).then_inc(S["kh_sub"].sem, 1)
                wait("e", i, 1)
                V.tensor_tensor(tile["qh"][:, :], tile["q"][:, :], tile["e"][:, :], ALU.mult).then_inc(S["qh"].sem, 1)
                V.tensor_copy(tile["dec"][:, 0:PT], tile["e"][:, 0:PROMPT].rearrange("p (t n) -> p t n", n=P)[:, :, P - 1])
                V.tensor_copy(tile["dec"][:, PT:PT + STREAMS],
                              tile["e"][:, PROMPT:T].rearrange("p (s n) -> p s n", n=STREAM_T)[:, :, STREAM_T - 1]
                              ).then_inc(S["dec"].sem, 1)
                wait("qh", i, 1)
                for s in range(STREAMS):
                    last = V.tensor_copy(tile["qz"][:, s, s * STREAM_T:(s + 1) * STREAM_T],
                                         tile["qh"][:, PROMPT + s * STREAM_T:PROMPT + (s + 1) * STREAM_T])
                last.then_inc(S["qz"].sem, 1)
                wait("kh_exp", i, 1)
                V.tensor_tensor(tile["c0"][:, :], tile["c0"][:, :], tile["k"][:, :], ALU.mult).then_inc(S["kh"].sem, 1)
                if not first:
                    apply_rms(K, i - 1)

            def chain_tail(K, p):
                n, dv = K["n"], K["dv"]
                S, tile = SIG[n], att[n]
                per_job = 512 // dv

                def wait(name, it, k):
                    dve.wait_ge(S[name].sem, S[name].at(it, k))

                wait("kt_pe", p, 3)
                v8 = tile["v"][:, PT, :].unsqueeze(1).to_broadcast([P, STREAMS, dv])
                own = own_stream[:, :].unsqueeze(2).to_broadcast([P, STREAMS, dv])
                V.tensor_tensor(tile["vz"][:, :, :], v8, own, ALU.mult).then_inc(S["vz"].sem, 1)
                for c in range(PT):
                    jb, x = c // per_job, c % per_job
                    kv = bank[(5, 6, 3, 4)[jb]][:, x * dv:(x + 1) * dv]
                    if x == 0:
                        wait("kvp_pe", p, jb + 1)
                    if c == 0:
                        wait("dec", p, 1)
                        V.tensor_copy(tile["chain"][:, 0, :], kv).then_inc(S["chain"].sem, 1)
                    else:
                        wait("chain", p, c)
                        V.scalar_tensor_tensor(tile["chain"][:, c, :], tile["chain"][:, c - 1, :], tile["dec"][:, c:c + 1], kv,
                                               ALU.mult, ALU.add).then_inc(S["chain"].sem, 1)
                wait("odec_pe", p, 1)
                V.scalar_tensor_tensor(tile["v"][:, PT, :], tile["v"][:, PT, :], tile["dot"][:, PT:NT], bank[7][:, 0:dv],
                                       ALU.mult, ALU.add).then_inc(S["o_add"].sem, 1)
                for s in range(STREAMS):
                    jb, x = s // per_job, s % per_job
                    kv = bank[((3, 4) if n == "h" else (5, 6, 3, 4))[jb]][:, x * dv:(x + 1) * dv]
                    if x == 0:
                        wait("kvd_pe", p, jb + 1)
                    V.scalar_tensor_tensor(tile["s0"][:, s, :], tile["s0"][:, s, :], tile["dec"][:, PT + s:PT + s + 1], kv,
                                           ALU.mult, ALU.add).then_inc(S["s0new"].sem, 1)

            def add_diagonal(K, p):
                n, dv = K["n"], K["dv"]
                S, tile = SIG[n], att[n]
                per_job = 512 // dv
                for c in range(PT):
                    jb, x = c // per_job, c % per_job
                    if x == 0:
                        dve.wait_ge(S["o_pe"].sem, S["o_pe"].at(p, jb + 1))
                    V.scalar_tensor_tensor(tile["v"][:, c, :], tile["v"][:, c, :], tile["dot"][:, c:c + 1],
                                           bank[6 + jb % 2][:, x * dv:(x + 1) * dv], ALU.mult, ALU.add).then_inc(S["o_add"].sem, 1)

            def gate(K, p):
                n, dv = K["n"], K["dv"]
                S, tile = SIG[n], att[n]
                g = tm[:, :, bass.ds(p * dv, dv)]
                dve.wait_ge(S["g_act"].sem, S["g_act"].at(p, 1))
                if n == "h":
                    V.tensor_tensor(g, g, tile["gt"][:, :, :], ALU.mult).then_inc(S["gated"].sem, 1)
                    dve.wait_ge(S["gated"].sem, S["gated"].at(p, 1))
                V.tensor_tensor(g, g, tile["norm"][:, :].unsqueeze(1).to_broadcast([P, NT, dv]), ALU.mult).then_inc(S["gated"].sem, 1)

            def apply_gate(K, p):
                dv, S, tile = K["dv"], SIG[K["n"]], att[K["n"]]
                g = tm[:, :, bass.ds(p * dv, dv)]
                dve.wait_ge(S["gated"].sem, S["gated"].at(p, S["gated"].per))
                dve.wait_ge(S["o_add"].sem, S["o_add"].at(p, NT))
                V.tensor_tensor(g, g, tile["v"][:, :, :], ALU.mult).then_inc(S["gated_o"].sem, 1)

            def apply_rms(K, p):
                dv, S, tile = K["dv"], SIG[K["n"]], att[K["n"]]
                g = tm[:, :, bass.ds(p * dv, dv)]
                dve.wait_ge(S["rms"].sem, S["rms"].at(p, 1))
                V.reciprocal(tile["rstd"][:, :], tile["rms"][:, :]).then_inc(S["rstd"].sem, 1)
                dve.wait_ge(S["gated_o"].sem, S["gated_o"].at(p, 1))
                dve.wait_ge(S["rstd"].sem, S["rstd"].at(p, 1))
                V.tensor_tensor(g, g, tile["rstd"][:, :].unsqueeze(2).to_broadcast([P, NT, dv]), ALU.mult
                                ).then_inc(S["final"].sem, 1)

            def out_projection(layer):
                for t in range(2):
                    take_transposed(t, w_job(layer, "o", t))
                dve.wait_ge(lnrow_in, 32 * (2 * layer + 1))
                for t in range(NT):
                    for half in range(2):
                        if half == 0:
                            dve.wait_ge(res_io[t], (16, 48)[layer])
                        m = (layer * NT + t) * 2 + half
                        dve.wait_ge(w_done, m + 1)
                        x = tm[:, t, half * 512:(half + 1) * 512]
                        V.scalar_tensor_tensor(x, x, ALPHA, bank[6 + half][:, :], ALU.mult, ALU.add).then_inc(w_added, 1)
                        for x in O_AHEAD[t] if half == 0 else ():
                            take_transposed(x, w_job(layer, "o", x))
                    if t >= 1:
                        take_transposed(t - 1, w_job(layer, "n", t - 1))
                        scale_residual(t - 1, layer)
                    dve.wait_ge(w_added, m + 1)
                    ln_stats(t, 2 * layer * NT + t)
                    ln_apply(t, layer)

            def scale_residual(t, layer):
                V.tensor_scalar(tm[:, t, :], tm[:, t, :], ALPHA, None, ALU.mult).then_inc(FSIG["added"].sem, 1)

            def ffn(layer):
                F = {k: v.layer(layer, NFF) for k, v in FSIG.items()}
                DN, AD = ffn_sums(layer)

                def wait(name, f, k):
                    dve.wait_ge(F[name].sem, F[name].at(f, k))

                dve.wait_ge(DN.sem, DN.at(0, 0))
                V.tensor_copy(params[:, :, :], bank[3][:, 0:NFF * ROWS].rearrange("p (f r) -> p f r", r=ROWS)).then_inc(params_rd, 1)
                dve.wait_ge(ln_done, (2 * layer + 1) * NT)
                for u in range(2):
                    V.memset(ax[u][:, 0:2], 0.0)
                take_transposed(NT - 1, w_job(layer, "n", NT - 1))
                scale_residual(NT - 1, layer)
                dve.wait_ge(params_rd, layer + 1)

                def param(f, r):
                    return params[:, bass.ds(f, 1), 2 * STREAMS + r]

                def conv(f, u):
                    dec = ax[u][:, 2 + PROMPT:].rearrange("p (s w) -> p s w", s=STREAMS)
                    V.tensor_copy(dec[:, :, 0:2], params[:, bass.ds(f, 1), 0:2 * STREAMS].rearrange("p o (s w) -> p (o s) w", s=STREAMS)
                                  ).then_inc(F["prev"].sem, 1)
                    wait("a_out", f, 3)
                    wait("prev", f, 1)
                    parts = [(cv[u][:, 0:PROMPT], lambda j: ax[u][:, j:j + PROMPT]),
                             (cv[u][:, PROMPT:T].rearrange("p (s w) -> p s w", s=STREAMS), lambda j: dec[:, :, j:j + STREAM_T])]
                    for j in range(3):
                        for x, (dst, tap) in enumerate(parts):
                            if j == 0:
                                ins = V.tensor_scalar(dst, tap(0), param(f, 0), param(f, 3), ALU.mult, ALU.add)
                            else:
                                ins = V.scalar_tensor_tensor(dst, tap(j), param(f, j), dst, ALU.mult, ALU.add)
                            if x == 1:
                                ins.then_inc(F["conv"].sem, 1)
                        if j < 2:
                            wait("conv", f, j + 1)

                def keep_tail(f, u):
                    dec = ax[u][:, 2 + PROMPT:].rearrange("p (s w) -> p s w", s=STREAMS)
                    V.tensor_copy(tails[:, bass.ds(f, 1), 0:2], ax[u][:, PROMPT:PROMPT + 2].unsqueeze(1)).then_inc(F["tail"].sem, 1)
                    V.tensor_copy(tails[:, bass.ds(f, 1), 2:TAILS].rearrange("p o (s w) -> p (o s) w", s=STREAMS),
                                  dec[:, :, STREAM_T:STREAM_T + 2]).then_inc(F["tail"].sem, 1)

                def multiply(f, u):
                    wait("gelu", f, 1)
                    for c in range(NC):
                        wait("b_pe", f, c + 1)
                        x = cv[u][:, c * CH:(c + 1) * CH]
                        V.tensor_tensor(x, x, bank[3 + c][:, 0:CH], ALU.mult).then_inc(F["mult"].sem, 1)

                def split(f, u, g):
                    wait("h_hi", f, 1)
                    V.tensor_tensor(h_lo[g][u][:, :], cv[u][:, :], h_hi[g][u][:, :].bitcast(F32), ALU.subtract
                                    ).then_inc(F["h_lo"].sem, 1)

                def add_down(j, t, between=None):
                    for n in range(2):
                        dve.wait_ge(DN.sem, DN.at(j, 2 * t + n + 1))
                        x = tm[:, t, n * 512:(n + 1) * 512]
                        V.tensor_tensor(x, x, bank[6 + n][:, :], ALU.add).then_inc(AD.sem, 1)
                        if between and n == 0:
                            between(t)

                def group(j, g, down):
                    for u in range(2):
                        f = j * 2 + u
                        conv(f, u)
                        keep_tail(f, u)
                        multiply(f, u)
                        if u == 0:
                            split(f, u, g)
                    if down:
                        for t in range(NT):
                            if t == 0:
                                dve.wait_ge(AD.sem, AD.at(j - 1, 0))
                            add_down(j - 1, t)
                    split(j * 2 + 1, 1, g)

                group(0, 0, False)
                with dve.Fori(0, GROUPS // 2 - 1) as pair:
                    j = pair * 2 + 1
                    group(j, 1, True)
                    group(j + 1, 0, True)
                group(GROUPS - 2, 1, True)
                group(GROUPS - 1, 0, False)
                dve.wait_ge(AD.sem, AD.at(GROUPS - 2, 0))
                dve.wait_ge(lnrow_in, 32 * (2 * layer + 2))
                n0 = (2 * layer + 1) * NT

                def scale_centered(t):
                    dve.wait_ge(ln_sqrt, n0 + t + 1)
                    V.reciprocal(inv_std[:, t:t + 1], std[:, t:t + 1]).then_inc(ln_std, 1)
                    dve.wait_ge(ln_std, n0 + t + 1)
                    dve.wait_ge(ln_centered, layer * NT + t + 1)
                    V.scalar_tensor_tensor(tm[:, t, :], tm[:, t, :], inv_std[:, t:t + 1], ln_ffn[0][:, :], ALU.mult, ALU.mult
                                           ).then_inc(ln_scaled, 1)

                def between(t):
                    if t >= 1:
                        scale_centered(t - 1)
                    if layer == 0 and t >= 2:
                        if t == 2:
                            dve.wait_ge(tails_dma, 32)
                        take_transposed(t - 2, JOB_G + 2 * (t - 2))

                for t in range(NT):
                    add_down(GROUPS - 2, t, between)
                    dve.wait_ge(AD.sem, AD.at(GROUPS - 2, 2 * t + 2))
                    ln_stats(t, n0 + t)
                    dve.wait_ge(ln_moments, n0 + t + 1)
                    V.tensor_scalar(neg_mean[:, t:t + 1], moments[:, t, 0:1], -1.0, None, ALU.mult).then_inc(ln_neg, 1)
                scale_centered(NT - 1)
                if layer == 0:
                    for t in (NT - 2, NT - 1):
                        take_transposed(t, JOB_G + 2 * t)

            V.memset(ones[:, :], 1.0)
            V.memset(eps_ln[:, :], LN_EPS)
            V.memset(eps_rms[:, :], RMS_EPS).then_inc(start_dve, 1)
            for t in range(NT):
                take_transposed(t, 2 * t, 6)
            dve.wait_ge(const_in, 16 * 7)
            V.tensor_copy(level_mask[:, :], level_f32[:, :])
            V.tensor_copy(keep[:, :], keep_f32[:, :])
            h = att["h"]
            V.reduce_max(h["lbs"][:, :, :], h["lb"][:, :, :], AX.X).then_inc(prep, 1)
            dve.wait_ge(prep, 1)
            V.tensor_tensor(h["lbx"][:, :, :], h["lb"][:, :, :], h["lbs"][:, :, :].to_broadcast([P, HEADS_H, 3]), ALU.subtract
                            ).then_inc(prep, 1)
            dve.wait_ge(prep, 3)
            V.reduce_sum(h["lbs"][:, :, :], h["lbx"][:, :, :], AX.X).then_inc(prep, 1)
            dve.wait_ge(prep, 4)
            V.reciprocal(h["span"][:, :, :], h["lbs"][:, :, :]).then_inc(prep, 1)
            dve.wait_ge(prep, 5)
            V.tensor_tensor(h["floor"][:, :, :], h["span"][:, :, :], h["lbx"][:, :, 0:1], ALU.mult).then_inc(prep, 1)
            dve.wait_ge(prep, 6)
            V.tensor_scalar(h["span"][:, :, :], h["floor"][:, :, :], -1.0, 1.0, ALU.mult, ALU.add).then_inc(prep, 1)
            dve.wait_ge(prep, 7)
            dve.wait_ge(start_pool, 1)
            attention(KIND["h"], 0, True, False)
            with dve.Fori(1, HEADS_H) as i:
                attention(KIND["h"], i, False, False)
            attention(KIND["h"], HEADS_H, False, True)
            out_projection(0)
            ffn(0)
            dve.wait_ge(const_in, 16 * 9)
            dve.wait_ge(start_pool, 2)
            attention(KIND["g"], 0, True, False)
            with dve.Fori(1, HEADS_G) as i:
                attention(KIND["g"], i, False, False)
            attention(KIND["g"], HEADS_G, False, True)
            out_projection(1)
            ffn(1)


_INS = ["x_prompt", "x_sample", "state_hgrn", "state_gla", "state_ffn_conv", "lb_param", "hgrn_w_in", "hgrn_w_out",
        "hgrn_norm_g", "gla_w_in", "gla_w_gk2", "gla_b_gk2", "gla_w_out", "gla_norm_g", "ln_mix_g", "ln_mix_b",
        "ffn_w_up", "ffn_conv_w", "ffn_conv_b", "ffn_w_down", "ln_ffn_g", "ln_ffn_b"]
_OUTS = [("y_prompt", (1, PROMPT, D)), ("y_sample", (STREAMS, STREAM_T, D)),
         ("hgrn_p", (1, 1, HEADS_H, P, DV_H)), ("hgrn_s", (1, STREAMS, HEADS_H, P, DV_H)),
         ("gla_p", (1, 1, HEADS_G, P, DV_G)), ("gla_s", (1, STREAMS, HEADS_G, P, DV_G)),
         ("conv_p", (2, 1, 2, FF)), ("conv_s", (2, STREAMS, 2, FF))]


def kernel(**inputs):
    import numpy as _np
    import concourse.bacc as _bacc
    from concourse import mybir as _mybir
    from concourse.bass_utils import run_bass_kernel_spmd as _run

    key = _np.arange(P)[:, None]
    level = _np.zeros((P, NL * 64), _np.float32)
    for x, m in enumerate(LEVELS):
        block_of_query = _np.arange(64)[None, :] // m
        level[:, x * 64:(x + 1) * 64] = (key // (2 * m) == block_of_query) & (key % (2 * m) < m)
    keep = _np.ones((P, T), _np.float32)
    keep[:, 0:PROMPT:P] = 0
    keep[:, PROMPT:T:STREAM_T] = 0
    consts = {
        "c_ident": _np.eye(P, dtype=_np.float32), "c_level": level, "c_keep": keep,
        "c_stream": (key // STREAM_T == _np.arange(STREAMS)[None, :]).astype(_np.float32),
    }

    nc = _bacc.Bacc("TRN2", target_bir_lowering=False, num_devices=1, dynamic_dma_scratch_size=1024)
    arrays, ins, outs = {}, {}, {}
    for name in _INS:
        arrays[f"in_{name}"] = _np.ascontiguousarray(inputs[name])
        ins[name] = nc.dram_tensor(f"in_{name}", arrays[f"in_{name}"].shape, _mybir.dt.float32, kind="ExternalInput").ap()
    for name, a in consts.items():
        arrays[f"in_{name}"] = a
        ins[name] = nc.dram_tensor(f"in_{name}", a.shape, _mybir.dt.from_np(a.dtype), kind="ExternalInput").ap()
    for name, shape in _OUTS:
        outs[name] = nc.dram_tensor(f"out_{name}", shape, _mybir.dt.float32, kind="ExternalOutput").ap()
    build(nc, ins, outs)
    r = _run(nc, [arrays], core_ids=[0])
    return tuple(r.results[0][f"out_{name}"] for name, _ in _OUTS)
```
